# Optimizing a Trainium2 kernel written in Bass

```python
import math
import jax, jax.numpy as jnp
from jax import lax
import numpy as np

D_MODEL = 1024
BATCH = 1
SEQ = 4096
DEPTH = 1

N_META = 16
N_Q_HEADS = 8
N_KV_HEADS = 2
HEAD_DIM = 64
Q_GROUP = N_Q_HEADS // N_KV_HEADS
ATTN_DIM = N_Q_HEADS * HEAD_DIM
KV_DIM = N_KV_HEADS * HEAD_DIM
WINDOW = 128
BLK = 128
PAD = BLK - N_META
N_BUCKETS = 32
MAX_DISTANCE = 128
CONV_CH = D_MODEL // 2
CONV_W = 3
IN_PROJ = ATTN_DIM + 2 * KV_DIM + 3 * CONV_CH
MIX_DIM = ATTN_DIM + CONV_CH
SPLITS = (ATTN_DIM, ATTN_DIM + KV_DIM, ATTN_DIM + 2 * KV_DIM,
          ATTN_DIM + 2 * KV_DIM + CONV_CH, ATTN_DIM + 2 * KV_DIM + 2 * CONV_CH)
N_GROUPS = 4
EXPERTS_PER_GROUP = 8
N_EXPERTS = N_GROUPS * EXPERTS_PER_GROUP
TOP_K = 2
D_EXPERT = D_MODEL // 2
MOE_BLK = 128
EPS = 1e-6
NEG_INF = -1e30

kernel_name = 'hymba_swa_sink_shortconv_hier_moe'

def rms_norm(x, g):
    xf = x.astype(jnp.float32)
    y = xf * lax.rsqrt(jnp.mean(xf * xf, axis=-1, keepdims=True) + EPS)
    return y.astype(x.dtype) * g

def t5_causal_bucket(n):
    max_exact = N_BUCKETS // 2
    nf = jnp.maximum(n, 1).astype(jnp.float32)
    large = max_exact + (jnp.log(nf / max_exact) / math.log(MAX_DISTANCE / max_exact)
                         * (N_BUCKETS - max_exact)).astype(jnp.int32)
    large = jnp.minimum(large, N_BUCKETS - 1)
    return jnp.where(n < max_exact, n, large)

def band_bias_and_mask(rel_bias, n_blocks):
    qi = jnp.arange(BLK)[:, None]
    sj = jnp.arange(2 * BLK)[None, :]
    dist = BLK + qi - sj
    band = (dist >= 0) & (dist < WINDOW)
    bucket = t5_causal_bucket(jnp.maximum(dist, 0))
    bias = jnp.transpose(rel_bias[bucket].astype(jnp.float32), (2, 0, 1))
    bias = bias.reshape(N_KV_HEADS, Q_GROUP, BLK, 2 * BLK)
    key_pos = (jnp.arange(n_blocks)[:, None, None] - 1) * BLK + sj[None]
    mask = band[None] & (key_pos >= PAD)
    return bias, mask

def sliding_window_sink_attention(q, k, v, sinks, rel_bias):
    bsz, seq = q.shape[0], q.shape[1]
    lp = seq + PAD
    nb = lp // BLK
    pad = ((0, 0), (PAD, 0), (0, 0), (0, 0))
    q = jnp.pad(q, pad).reshape(bsz, nb, BLK, N_KV_HEADS, Q_GROUP, HEAD_DIM)
    k = jnp.pad(k, pad).reshape(bsz, nb, BLK, N_KV_HEADS, HEAD_DIM)
    v = jnp.pad(v, pad).reshape(bsz, nb, BLK, N_KV_HEADS, HEAD_DIM)
    prev = lambda t: jnp.pad(t, ((0, 0), (1, 0), (0, 0), (0, 0), (0, 0)))[:, :-1]
    kw = jnp.concatenate([prev(k), k], axis=2)
    vw = jnp.concatenate([prev(v), v], axis=2)
    bias, mask = band_bias_and_mask(rel_bias, nb)
    s = jnp.einsum('bnqkgd,bnskd->bnkgqs', q, kw).astype(jnp.float32) * (HEAD_DIM ** -0.5) + bias
    s = jnp.where(mask[None, :, None, None], s, NEG_INF)
    sink = sinks.astype(jnp.float32).reshape(1, 1, N_KV_HEADS, Q_GROUP, 1, 1)
    m = jnp.maximum(jnp.max(s, axis=-1, keepdims=True), sink)
    p = jnp.exp(s - m)
    p = p / (jnp.sum(p, axis=-1, keepdims=True) + jnp.exp(sink - m))
    o = jnp.einsum('bnkgqs,bnskd->bnqkgd', p.astype(v.dtype), vw)
    return o.reshape(bsz, lp, ATTN_DIM)[:, PAD:]

def short_gated_conv(b_gate, c_gate, h, conv_w):
    u = c_gate * h
    y = lax.conv_general_dilated(u, conv_w[:, None, :].astype(u.dtype), (1,), [(CONV_W - 1, 0)],
                                 dimension_numbers=('NWC', 'WIO', 'NWC'),
                                 feature_group_count=CONV_CH)
    return b_gate * y

def hierarchical_moe(xt, w_gr, b_gr, w_er, b_er, w_g, w_u, w_d):
    n_tok = xt.shape[0]
    xf = xt.astype(jnp.float32)
    g_prob = jax.nn.softmax(xf @ w_gr.astype(jnp.float32) + b_gr.astype(jnp.float32), axis=-1)
    g_p, g_idx = lax.top_k(g_prob, 1)
    e_logits = jnp.einsum('td,dge->tge', xf, w_er.astype(jnp.float32)) + b_er.astype(jnp.float32)
    e_logits = jnp.take_along_axis(e_logits, g_idx[:, :, None], axis=1)[:, 0]
    e_val, e_idx = lax.top_k(e_logits, TOP_K)
    gates = g_p * jax.nn.softmax(e_val, axis=-1)
    expert_id = g_idx * EXPERTS_PER_GROUP + e_idx
    n_asg = n_tok * TOP_K
    eid = expert_id.reshape(n_asg)
    order = jnp.argsort(eid)
    eid_s = eid[order]
    tok_s = order // TOP_K
    gate_s = gates.reshape(n_asg)[order]
    counts = jnp.bincount(eid, length=N_EXPERTS)
    padded = (counts + MOE_BLK - 1) // MOE_BLK * MOE_BLK
    pend = jnp.cumsum(padded)
    start = jnp.cumsum(counts) - counts
    dest = (pend - padded)[eid_s] + jnp.arange(n_asg) - start[eid_s]
    n_blocks = -(-n_asg // MOE_BLK) + N_EXPERTS
    xbuf = jnp.zeros((n_blocks * MOE_BLK, D_MODEL), xt.dtype).at[dest].set(xt[tok_s])
    block_e = jnp.minimum(jnp.searchsorted(pend, jnp.arange(n_blocks) * MOE_BLK, side='right'),
                          N_EXPERTS - 1)

    def expert_block(args):
        xb, e = args
        return (jax.nn.silu(xb @ w_g[e]) * (xb @ w_u[e])) @ w_d[e]

    ybuf = lax.map(expert_block, (xbuf.reshape(n_blocks, MOE_BLK, D_MODEL), block_e))
    y = ybuf.reshape(n_blocks * MOE_BLK, D_MODEL)[dest] * gate_s[:, None].astype(xt.dtype)
    return jax.ops.segment_sum(y, tok_s, num_segments=n_tok)

def setup_inputs(seed: int = 0) -> dict:
    key = jax.random.key(seed)
    ks = jax.random.split(key, 20)
    f32 = jnp.float32

    def nrm(k, shape, scale):
        return jax.random.normal(k, shape, f32) * scale

    def gain(k, shape):
        return 1.0 + 0.02 * jax.random.normal(k, shape, f32)

    return {
        'x': nrm(ks[0], (BATCH, SEQ, D_MODEL), 1.0),
        'meta_tokens': nrm(ks[1], (N_META, D_MODEL), 1.0),
        'rel_bias': nrm(ks[2], (N_BUCKETS, N_Q_HEADS), 0.2),
        'mix_norm_g': gain(ks[3], (DEPTH, D_MODEL)),
        'w_in': nrm(ks[4], (DEPTH, D_MODEL, IN_PROJ), D_MODEL ** -0.5),
        'q_norm_g': gain(ks[5], (DEPTH, HEAD_DIM)),
        'k_norm_g': gain(ks[6], (DEPTH, HEAD_DIM)),
        'attn_sinks': nrm(ks[7], (DEPTH, N_Q_HEADS), 0.5),
        'conv_w': nrm(ks[8], (DEPTH, CONV_W, CONV_CH), CONV_W ** -0.5),
        'attn_out_norm_g': gain(ks[9], (DEPTH, ATTN_DIM)),
        'conv_out_norm_g': gain(ks[10], (DEPTH, CONV_CH)),
        'w_out': nrm(ks[11], (DEPTH, MIX_DIM, D_MODEL), MIX_DIM ** -0.5),
        'ffn_norm_g': gain(ks[12], (DEPTH, D_MODEL)),
        'w_group_router': nrm(ks[13], (DEPTH, D_MODEL, N_GROUPS), D_MODEL ** -0.5),
        'b_group_router': nrm(ks[14], (DEPTH, N_GROUPS), 0.01),
        'w_expert_router': nrm(ks[15], (DEPTH, D_MODEL, N_GROUPS, EXPERTS_PER_GROUP), D_MODEL ** -0.5),
        'b_expert_router': nrm(ks[16], (DEPTH, N_GROUPS, EXPERTS_PER_GROUP), 0.01),
        'w_gate': nrm(ks[17], (DEPTH, N_EXPERTS, D_MODEL, D_EXPERT), D_MODEL ** -0.5),
        'w_up': nrm(ks[18], (DEPTH, N_EXPERTS, D_MODEL, D_EXPERT), D_MODEL ** -0.5),
        'w_down': nrm(ks[19], (DEPTH, N_EXPERTS, D_EXPERT, D_MODEL), D_EXPERT ** -0.5),
    }

def reference(x, meta_tokens, rel_bias, mix_norm_g, w_in, q_norm_g, k_norm_g, attn_sinks, conv_w,
              attn_out_norm_g, conv_out_norm_g, w_out, ffn_norm_g, w_group_router, b_group_router,
              w_expert_router, b_expert_router, w_gate, w_up, w_down):
    bsz = x.shape[0]
    meta = jnp.broadcast_to(meta_tokens.astype(x.dtype)[None], (bsz, N_META, D_MODEL))
    h = jnp.concatenate([meta, x], axis=1)
    seq = h.shape[1]
    for l in range(DEPTH):
        hn = rms_norm(h, mix_norm_g[l])
        proj = hn @ w_in[l]
        q, k, v, cb, cc, ch = jnp.split(proj, SPLITS, axis=-1)
        q = rms_norm(q.reshape(bsz, seq, N_Q_HEADS, HEAD_DIM), q_norm_g[l])
        k = rms_norm(k.reshape(bsz, seq, N_KV_HEADS, HEAD_DIM), k_norm_g[l])
        v = v.reshape(bsz, seq, N_KV_HEADS, HEAD_DIM)
        a = sliding_window_sink_attention(q, k, v, attn_sinks[l], rel_bias)
        c = short_gated_conv(cb, cc, ch, conv_w[l])
        mixed = jnp.concatenate([rms_norm(a, attn_out_norm_g[l]),
                                 rms_norm(c, conv_out_norm_g[l])], axis=-1)
        h = h + mixed @ w_out[l]
        hn = rms_norm(h, ffn_norm_g[l])
        y = hierarchical_moe(hn.reshape(bsz * seq, D_MODEL), w_group_router[l], b_group_router[l],
                             w_expert_router[l], b_expert_router[l], w_gate[l], w_up[l], w_down[l])
        h = h + y.reshape(bsz, seq, D_MODEL)
    return h[:, N_META:]


_drawn_inputs = setup_inputs


def setup_inputs(seed=0):
    import zlib

    import numpy as np

    out = dict(_drawn_inputs(seed))
    spreads = {}
    factors = {'q_norm_g': 2.948,
     'k_norm_g': 2.941,
     'attn_sinks': 64.0,
     'attn_out_norm_g': 11.251,
     'conv_out_norm_g': 10.965,
     'b_group_router': 25.205,
     'b_expert_router': 21.337,
     'ffn_norm_g': 6.099}
    for name, (base, spread) in spreads.items():
        noise = np.random.default_rng([zlib.crc32(name.encode()), seed]).standard_normal(out[name].shape)
        drawn = base * np.exp(spread * noise) if base else spread * noise
        out[name] = __import__('jax').numpy.asarray(drawn.astype(out[name].dtype))
    for name, factor in factors.items():
        out[name] = (out[name] * factor).astype(out[name].dtype)
    return out
```

```python
import math
from contextlib import ExitStack

import numpy as np

import concourse.bass as bass
from concourse import mybir

ALU = mybir.AluOpType
ACT = mybir.ActivationFunctionType
F32 = mybir.dt.float32
F32R = mybir.dt.float32r
F16 = mybir.dt.float16
BF16 = mybir.dt.bfloat16
I32 = mybir.dt.int32
AX = mybir.AxisListType.X
RMAX = bass.bass_isa.ReduceOp.max

P = 128
D = 1024
KD = D // P
SEQ = 4096
TILES = SEQ // P
N_META = 16
HEADS, KV, HD = 8, 2, 64
AD = HEADS * HD
CC = 512
IN = 2304
O_K, O_B, O_C, O_H = 512, 768, 1280, 1792
BUCKETS = 32
GROUPS, PER_GROUP, E = 4, 8, 32
DE = 512
KE = DE // P
CAP = SEQ
EPS = 1e-6
NEG = -1e30
XS = 256.0
BW = 384

C_ID, C_TRI, C_ONE, C_W32, C_SLOT, C_W4, C_TOK, C_JUNK, C_EPS = 0, 128, 256, 384, 416, 448, 452, 453, 454
CW = 456


def constants():
    c = np.zeros((P, CW), np.float32)
    c[:, C_ID:C_ID + P] = np.eye(P)
    c[:, C_TRI:C_TRI + P] = np.triu(np.ones((P, P)), 1)
    c[:, C_ONE:C_ONE + P] = 1
    c[:, C_W32:C_W32 + E] = np.arange(E, 0, -1)
    c[:, C_SLOT:C_SLOT + E] = np.arange(E) * CAP
    c[:, C_W4:C_W4 + GROUPS] = np.arange(GROUPS, 0, -1)
    c[:, C_TOK] = np.arange(P)
    c[:, C_JUNK] = SEQ + np.arange(P)
    c[:, C_EPS] = EPS
    dist = 2 * P - 1 - np.arange(BW)
    half = BUCKETS // 2
    n = np.maximum(dist, 1).astype(np.float32)
    large = half + (np.log(n / half) / np.float32(math.log(P / half)) * (BUCKETS - half)).astype(np.int32)
    bucket = np.where(dist < half, np.maximum(dist, 0), np.minimum(large, BUCKETS - 1))
    hot = np.zeros((BUCKETS + 1, BW), np.float32)
    hot[bucket, np.arange(BW)] = 1
    hot[BUCKETS] = np.where((dist >= 0) & (dist < P), 0, NEG)
    return c, hot


class Signal:

    def __init__(self, sem, per=1, first=1):
        self.sem, self.per, self.first = sem, per, first

    def at(self, t, part=None):
        part = self.per if part is None else part
        if isinstance(t, int):
            return self.per * (t - self.first) + part
        return t * self.per + (part - self.per * self.first)


def after(eng, signal, t, part=None):
    value = signal.at(t, part)
    if not isinstance(value, int) or value > 0:
        eng.wait_ge(signal.sem, value)


def hold(eng, passed):
    eng.sem_inc(passed, 1)


def build(nc, x, meta_tokens, rel_bias, mix_norm_g, w_in, q_norm_g, k_norm_g, attn_sinks, conv_w,
          attn_out_norm_g, conv_out_norm_g, w_out, ffn_norm_g, w_group_router, b_group_router,
          w_expert_router, b_expert_router, w_gate, w_up, w_down, consts, onehot, out):
    x2 = x.rearrange("b s d -> (b s) d")
    table = nc.dram_tensor("slot_table", [E * CAP, 2], I32).ap()
    hn_dram = nc.dram_tensor("hn_rows", [SEQ + P, D], F32).ap()
    u_dram = nc.dram_tensor("u_rows", [(TILES + 1) * P, CC], F32).ap()
    band_dram = nc.dram_tensor("band_rows", [P, HEADS * BW], F32).ap()

    def bcast(a, n, offset=0):
        return bass.AP(a.tensor, a.offset + offset, [[0, P], [1, n]])

    with ExitStack() as keep:
        def ksb(name, shape, dt):
            return keep.enter_context(nc.sbuf_tensor(name, shape, dt))

        cst = ksb("cst", [P, CW], F32)
        ident = cst[:, C_ID:C_ID + P]
        blocks_of = ksb("blocks_of", [P, 2 * E], I32)
        psA, psB, psC, psD, psE, psF, psG, psH = (
            keep.enter_context(nc.psum_tensor(f"ps{c}", [P, 512], F32)) for c in "ABCDEFGH")
        with ExitStack() as ctx:
            mixer(nc, ctx, locals())
        with ExitStack() as ctx:
            experts(nc, ctx, locals())


def mixer(nc, ctx, env):
    (x2, meta_tokens, rel_bias, mix_norm_g, w_in, q_norm_g, k_norm_g, attn_sinks, conv_w,
     attn_out_norm_g, conv_out_norm_g, w_out, ffn_norm_g, w_group_router, b_group_router,
     w_expert_router, b_expert_router, consts, onehot, out, table, hn_dram, u_dram, band_dram, bcast,
     cst, ident, blocks_of) = (env[n] for n in (
         "x2 meta_tokens rel_bias mix_norm_g w_in q_norm_g k_norm_g attn_sinks conv_w attn_out_norm_g "
         "conv_out_norm_g w_out ffn_norm_g w_group_router b_group_router w_expert_router b_expert_router "
         "consts onehot out table hn_dram u_dram band_dram bcast cst ident blocks_of").split())
    psA, psB, psC, psD, psE, psF, psG, psH = (env[f"ps{c}"] for c in "ABCDEFGH")

    def sb(name, shape, dt=F32):
        return ctx.enter_context(nc.sbuf_tensor(name, shape, dt))

    def sig(name, per=1, first=1):
        return Signal(ctx.enter_context(nc.semaphore(name)), per, first)

    wi_hi, wi_lo = sb("wi_hi", [P, KD, IN], F16), sb("wi_lo", [P, KD, IN], F16)
    wo_hi, wo_lo = sb("wo_hi", [P, KD, D], F16), sb("wo_lo", [P, KD, D], F16)
    w_rt = sb("w_rt", [P, KD, GROUPS + E])
    b_rt = sb("b_rt", [P, GROUPS + E])
    tri16, one16 = sb("tri16", [P, P], F16), sb("one16", [P, P], F16)
    g_ffn = sb("g_ffn", [P, D])
    w_cv = sb("w_cv", [P, 3, CC])
    bias = sb("bias", [P, HEADS, 2 * P])
    sinks = sb("sinks", [P, HEADS])
    g_mix, g_out = sb("g_mix", [P, KD]), sb("g_out", [P, KD])
    g_qk = sb("g_qk", [P, 2])
    pad_mask = sb("pad_mask", [1, 2, 2 * P])
    scale_w = sb("scale_w", [P, 8])
    inv_in, inv_out = scale_w[:, 4:5], scale_w[:, 5:6]
    xt, xn, xres = sb("xt", [P, D]), sb("xn", [P, D]), sb("xres", [P, D])
    xT_hi, xT_lo = sb("xT_hi", [P, KD, P], F16), sb("xT_lo", [P, KD, P], F16)
    dump = sb("dump", [P, D], BF16)
    stat = sb("stat", [P, 64])
    qsq, ksq = sb("qsq", [P, AD]), sb("ksq", [P, KV * HD])
    qn, kn, vst = sb("qn", [P, 4, KV, HD]), sb("kn", [P, KV * HD]), sb("vst", [P, KV * HD])
    qT, kT, V = sb("qT", [P, 4 * P]), sb("kT", [P, 2 * P]), sb("V", [P, 2, KV * HD])
    Cs, Bs, u = sb("Cs", [P, CC]), sb("Bs", [P, CC]), sb("u", [P, CC])
    um, yc = sb("um", [P, 2, CC]), sb("yc", [P, CC])
    prob, probT = sb("prob", [P, HEADS, 2 * P]), sb("probT", [P, HEADS, 2, P])
    a = sb("a", [P, AD])
    mT_hi, mT_lo = sb("mT_hi", [P, KD, P], F16), sb("mT_lo", [P, KD, P], F16)
    h, hn, hnT = sb("h", [P, D]), sb("hn", [P, D]), sb("hnT", [P, KD, P])
    lgb, lm, cand = sb("lgb", [P, GROUPS + E]), sb("lm", [P, E]), sb("cand", [P, E])
    oh4, pen4 = sb("oh4", [P, GROUPS]), sb("pen4", [P, GROUPS])
    hot1, hot2, rank = sb("hot1", [P, E]), sb("hot2", [P, E]), sb("rank", [P, E])
    both16 = sb("both16", [P, E], F16)
    running = sb("running", [P, E])
    rs = sb("rs", [P, 24])
    tok = sb("tok", [P, 1])
    slot = sb("slot", [P, 2], I32)
    entry = sb("entry", [P, 2, 2], I32)
    ss_x, r_x, ss_a, r_a, ss_c, r_c, ss_h, r_h = (stat[:, n:n + 1] for n in range(8))
    ln1 = [stat[:, 8 + n:9 + n] for n in range(4)]
    ss_q, ln_q, r_q = stat[:, 12:20], stat[:, 20:28], stat[:, 28:36]
    ss_k, ln_k, r_k = stat[:, 36:38], stat[:, 38:40], stat[:, 40:42]
    soft = sb("soft", [P, 48])
    top, ntop, psum_, sink_d, sink_e, den = (soft[:, 8 * n:8 * n + 8] for n in range(6))
    eps = cst[:, C_EPS:C_EPS + 1]

    ring = [h, hn, xres, xn]
    pieces = [("in", k, n * 768, 768) for k in range(KD) for n in range(3)]
    pieces += [("out", k, 0, D) for k in range(KD)]
    NP = len(pieces)

    def source(piece):
        kind, k, c0, n = piece
        w = w_in if kind == "in" else w_out
        return w[0, k * P:(k + 1) * P, c0:c0 + n]

    with ExitStack() as sctx:
        def sem(name):
            return sctx.enter_context(nc.semaphore(name))
        small_in, cst_in, hot_in = sem("small_in"), sem("cst_in"), sem("hot_in")
        w_slot = [sem(f"w_slot{n}") for n in range(4)]
        l1_done, hi_done, lo_done = sem("l1_done"), sem("hi_done"), sem("lo_done")
        dve_step, pool_step = sem("dve_step"), sem("pool_step")
        spread, band_ps, band_sb, band_out, band_in = (
            sem("spread"), sem("band_ps"), sem("band_sb"), sem("band_out"), sem("band_in"))
        filled, zeroed = sem("filled"), sem("zeroed")
        scaled = sem("scaled")
        l1 = sctx.enter_context(nc.sbuf_tensor("l1", [P, NP], F32))
        sI = sctx.enter_context(nc.sbuf_tensor("sI", [P, 8], I32))
        hot = xt[0:BUCKETS + 1, 0:BW]
        rb = xt[0:BUCKETS + 1, 512:520]
        rbx = a
        gk = qsq
        block = sctx.enter_context(nc.Block())

        @block.sync
        def _(sp):
            sp.dma_start(cst[:], consts).then_inc(cst_in, 16)
            sp.dma_start(hot, onehot).then_inc(hot_in, 16)
            sp.dma_start(rb[0:BUCKETS, :], rel_bias).then_inc(hot_in, 16)
            sp.dma_start(g_mix[:], mix_norm_g.rearrange("o (k p) -> p (o k)", p=P), allow_slow_non_contiguous=True).then_inc(small_in, 16)
            sp.dma_start(g_out[:, 0:4], attn_out_norm_g.rearrange("o (k p) -> p (o k)", p=P), allow_slow_non_contiguous=True).then_inc(small_in, 16)
            sp.dma_start(g_out[:, 4:8], conv_out_norm_g.rearrange("o (k p) -> p (o k)", p=P), allow_slow_non_contiguous=True).then_inc(small_in, 16)
            for half in range(2):
                sp.dma_start(gk[64 * half:64 * half + 64, 0:1], q_norm_g.rearrange("o d -> d o"), allow_slow_non_contiguous=True).then_inc(small_in, 16)
                sp.dma_start(gk[64 * half:64 * half + 64, 1:2], k_norm_g.rearrange("o d -> d o"), allow_slow_non_contiguous=True).then_inc(small_in, 16)
            for j in range(2 * NP):
                if j >= 4:
                    p = j - 4
                    if p < NP:
                        sp.wait_ge(l1_done, p + 1)
                    else:
                        sp.wait_ge(hi_done, p - NP + 1)
                        sp.wait_ge(lo_done, p - NP + 1)
                n = pieces[j % NP][3]
                sp.dma_start(ring[j % 4][:, 0:n], source(pieces[j % NP])).then_inc(w_slot[j % 4], 16)

        @block.scalar
        def _(act):
            act.preload_act_table_set("natural_log_exp_and_others")
            act.dma_start(sinks[:], bcast(attn_sinks, HEADS)).then_inc(small_in, 16)
            act.dma_start(b_rt[:, 0:GROUPS], bcast(b_group_router, GROUPS)).then_inc(small_in, 16)
            act.dma_start(b_rt[:, GROUPS:], bcast(b_expert_router, E)).then_inc(small_in, 16)
            act.dma_start(g_ffn[:], bcast(ffn_norm_g, D)).then_inc(small_in, 16)
            act.dma_start(w_cv[:].rearrange("p a c -> p (a c)"), bcast(conv_w, 3 * CC)).then_inc(small_in, 16)
            for k in range(KD):
                act.dma_start(w_rt[:, k, 0:GROUPS], w_group_router[0, k * P:(k + 1) * P, :]).then_inc(small_in, 16)
                act.dma_start(w_rt[:, k, GROUPS:], w_expert_router[0, k * P:(k + 1) * P].rearrange(
                    "p g e -> p (g e)")).then_inc(small_in, 16)
            act.wait_ge(small_in, 16 * 28)
            for j, (kind, k, _, n) in enumerate(pieces):
                g = (g_mix if kind == "in" else g_out)[:, k:k + 1]
                act.wait_ge(w_slot[j % 4], 16 * (j // 4 + 1))
                if j:
                    act.wait_ge(l1_done, j)
                nc.scalar.activation(dump[:, 0:n], ring[j % 4][:, 0:n], ACT.Abs, scale=g,
                                     accum_out=l1[:, j:j + 1]).then_inc(l1_done, 1)
            act.wait_ge(scaled, 1)
            for j, (kind, k, c0, n) in enumerate(pieces):
                q = NP + j
                g = (g_mix if kind == "in" else g_out)[:, k:k + 1]
                hi = (wi_hi if kind == "in" else wo_hi)[:, k, c0:c0 + n]
                act.wait_ge(w_slot[q % 4], 16 * (q // 4 + 1))
                nc.scalar.activation(hi, ring[q % 4][:, 0:n], ACT.Copy, scale=g).then_inc(hi_done, 1)

        @block.gpsimd
        def _(pool):
            pool.memset(probT[:], 0.0).then_inc(pool_step, 1)
            pool.memset(yc[:], 0.0).then_inc(pool_step, 1)
            pool.wait_ge(pool_step, 2)
            fill = probT[:].rearrange("p a b c -> p (a b c)").bitcast(I32).rearrange("p (r j w) -> p r j w", r=8, w=2)
            pool.iota(fill[:, :, :, 0], pattern=[[0, 8], [1, P]], base=SEQ, channel_multiplier=0).then_inc(pool_step, 1)
            pool.wait_ge(pool_step, 3)
            pool.dma_start(table.rearrange("(p r) w -> p (r w)", p=P),
                           fill.rearrange("p r j w -> p (r j w)")).then_inc(filled, 16)
            for c in range(2):
                pool.dma_start(hn_dram[SEQ:SEQ + P, c * CC:(c + 1) * CC], yc[:]).then_inc(zeroed, 16)
                pool.dma_start(out[SEQ:SEQ + P, c * CC:(c + 1) * CC], yc[:]).then_inc(zeroed, 16)
            pool.wait_ge(filled, 16)
            for n in range(2):
                pool.wait_ge(band_sb, 4 * n + 4)
                pool.dma_start(band_dram[:, n * 4 * BW:(n + 1) * 4 * BW],
                               probT[:].rearrange("p a b c -> p (a b c)")[:, 0:4 * BW]).then_inc(band_out, 16)
                pool.wait_ge(band_out, 16 * n + 16)
            pool.dma_start(bias[:], bass.AP(band_dram.tensor, band_dram.offset + P - 1,
                                            [[HEADS * BW - 1, P], [BW, HEADS], [1, 2 * P]])).then_inc(band_in, 16)
            pool.wait_ge(dve_step, 9)
            pool.partition_all_reduce(scale_w[:, 2:3], scale_w[:, 0:1], P, RMAX).then_inc(pool_step, 1)
            pool.partition_all_reduce(scale_w[:, 3:4], scale_w[:, 1:2], P, RMAX).then_inc(pool_step, 1)
            pool.wait_ge(zeroed, 64)
            pool.wait_ge(band_in, 16)

        @block.vector
        def _(dve):
            v = nc.vector
            steps = [0]

            def step(ins):
                steps[0] += 1
                ins.then_inc(dve_step, 1)
                dve.wait_ge(dve_step, steps[0])

            dve.wait_ge(cst_in, 16)
            dve.wait_ge(small_in, 16 * 28)
            step(v.tensor_copy(tri16[:], cst[:, C_TRI:C_TRI + P]))
            step(v.tensor_copy(one16[:], cst[:, C_ONE:C_ONE + P]))
            step(v.tensor_copy(running[:], cst[:, C_SLOT:C_SLOT + E]))
            step(v.tensor_copy(tok[:], cst[:, C_TOK:C_TOK + 1]))
            step(v.scalar_tensor_tensor(g_qk[:, 0:1], gk[:, 0:1], HD ** -0.5, gk[:, 1:2], ALU.mult, ALU.mult))
            step(v.memset(pad_mask[:], 0.0))
            step(v.memset(pad_mask[:, :, 0:P - N_META], NEG))
            dve.wait_ge(hot_in, 32)
            v.memset(rb[BUCKETS:BUCKETS + 1, :], 1.0).then_inc(spread, 1)
            dve.wait_ge(spread, 1)
            for n in range(2):
                if n:
                    dve.wait_ge(band_ps, 4)
                v.tensor_copy(rbx[0:BUCKETS + 1, :].rearrange("p (j c) -> p j c", j=4),
                              rb[:, 4 * n:4 * n + 4].unsqueeze(2).to_broadcast([BUCKETS + 1, 4, P])).then_inc(spread, 1)
                for j in range(4):
                    dve.wait_ge(band_ps, 4 * n + j + 1)
                    if n == 0 and j == 0:
                        dve.wait_ge(filled, 16)
                    if n and j == 0:
                        dve.wait_ge(band_out, 16)
                    v.tensor_copy(probT[:].rearrange("p a b c -> p (a b c)")[:, j * BW:(j + 1) * BW],
                                  [psA, psB, psC, psD][j][:, 0:BW]).then_inc(band_sb, 1)
            dve.wait_ge(l1_done, NP)
            step(v.tensor_reduce(scale_w[:, 0:1], l1[:, 0:3 * KD], AX, ALU.max))
            step(v.tensor_reduce(scale_w[:, 1:2], l1[:, 3 * KD:NP], AX, ALU.max))
            dve.wait_ge(pool_step, 5)
            step(v.tensor_scalar(sI[:, 0:2], scale_w[:, 2:4].bitcast(I32), 0x7F800000, None, ALU.bitwise_and))
            step(v.tensor_scalar(sI[:, 2:4], sI[:, 0:2], float(30 << 23), None, ALU.max))
            step(v.tensor_scalar(scale_w[:, 6:8].bitcast(I32), sI[:, 2:4], -1.0, float(268 << 23), ALU.mult, ALU.add))
            step(v.tensor_scalar(scale_w[:, 4:6].bitcast(I32), sI[:, 2:4], float(-(22 << 23)), None, ALU.add))
            step(v.tensor_scalar(g_mix[:], g_mix[:], scale_w[:, 6:7], None, ALU.mult))
            v.tensor_scalar(g_out[:], g_out[:], scale_w[:, 7:8], None, ALU.mult).then_inc(scaled, 1)
            dve.wait_ge(scaled, 1)
            for j, (kind, k, c0, n) in enumerate(pieces):
                q = NP + j
                g = (g_mix if kind == "in" else g_out)[:, k:k + 1]
                hi = (wi_hi if kind == "in" else wo_hi)[:, k, c0:c0 + n]
                lo = (wi_lo if kind == "in" else wo_lo)[:, k, c0:c0 + n]
                dve.wait_ge(w_slot[q % 4], 16 * (q // 4 + 1))
                dve.wait_ge(hi_done, j + 1)
                v.scalar_tensor_tensor(lo, ring[q % 4][:, 0:n], g, hi, ALU.mult, ALU.subtract).then_inc(lo_done, 1)

        @block.tensor
        def _(pe):
            pe.wait_ge(hot_in, 32)
            for n in range(2):
                pe.wait_ge(spread, 2 + n)
                for j in range(4):
                    if n:
                        pe.wait_ge(band_sb, j + 1)
                    nc.tensor.matmul([psA, psB, psC, psD][j][:, 0:BW], rbx[0:BUCKETS + 1, j * P:(j + 1) * P], hot,
                                     start=True, stop=True).then_inc(band_ps, 1)

    x_in, x_sq, x_rs, xn_s = sig("x_in", 16, 0), sig("x_sq", 1, 0), sig("x_rs", 2, 0), sig("xn_s", 1, 0)
    blank = sig("blank", 1, 0)
    xT_ps, xTh, xTl = sig("xT_ps", 2, 0), sig("xTh", 2, 0), sig("xTl", 2, 0)
    pq, pkv, pc, ph, pb = sig("pq"), sig("pkv", 1, 0), sig("pc", 1, 0), sig("ph", 1, 0), sig("pb")
    q_sq, q_ss, q_rs, q_n = sig("q_sq"), sig("q_ss"), sig("q_rs", 2), sig("q_n", 2)
    k_sq, k_ss, k_rs, k_n = sig("k_sq", 1, 0), sig("k_ss", 1, 0), sig("k_rs", 2, 0), sig("k_n", 1, 0)
    v_st, v_prev, v_cur = sig("v_st", 1, 0), sig("v_prev"), sig("v_cur", 1, 0)
    qT_ps, kT_ps, qT_s, k_prev, kT_s = (
        sig("qT_ps"), sig("kT_ps", 1, 0), sig("qT_s"), sig("k_prev"), sig("kT_s", 1, 0))
    c_sb, u_s, u_out, um_in, b_sb = (
        sig("c_sb", 1, 0), sig("u_s", 1, 0), sig("u_out", 16, 0), sig("um_in", 32), sig("b_sb"))
    s_ps, s_sb, n_top, p_sb, sink_ds, sink_es = (
        sig("s_ps", 4), sig("s_sb", 8), sig("n_top", 4), sig("p_sb", 8), sig("sink_ds"), sig("sink_es"))
    pT_ps, pT_act, pT_dve, den_s = sig("pT_ps", 4), sig("pT_act", 2), sig("pT_dve", 2), sig("den_s", 2)
    o_ps, a_s, a_sq, a_rs, a_n = sig("o_ps"), sig("a_s"), sig("a_sq"), sig("a_rs", 2), sig("a_n")
    cv, c_sq, c_rs, c_n = sig("cv", 6), sig("c_sq"), sig("c_rs", 2), sig("c_n")
    mT_ps, mTh, mTl = sig("mT_ps", 2), sig("mTh", 2), sig("mTl", 2)
    xres_in, h_ps, h_s, h_sq, h_rs, hn_s = (
        sig("xres_in", 16), sig("h_ps", 2), sig("h_s", 2), sig("h_sq"), sig("h_rs", 2), sig("hn_s"))
    rows_out = sig("rows_out", 32)
    hT_ps, hT_act, hT_dve = sig("hT_ps", 2), sig("hT_act"), sig("hT_dve")
    lg_ps, cnt_ps = sig("lg_ps"), sig("cnt_ps")
    R1, R2 = 18, 10
    rt1, rt2, rt_e = sig("rt1", R1), sig("rt2", R2), sig("rt_e", 2)
    listed = sig("listed", 32)
    dve_held, pool_held = sig("dve_held").sem, sig("pool_held").sem
    hot2_s, counted = sig("hot2_s"), sig("counted", 2)

    def schedule(eng, body):
        for t in range(-2, 3):
            body(t)
        with eng.Fori(3, TILES - 1) as t:
            body(t)
        for t in range(TILES - 1, TILES + 2):
            body(t)

    def live(t, lo, hi=TILES):
        return not isinstance(t, int) or lo <= t <= hi

    block = ctx.enter_context(nc.Block())

    @block.sync
    def _(sp):
        def body(t):
            if live(t + 2, 0):
                after(sp, xn_s, t + 1)
                if isinstance(t, int) and t == -2:
                    sp.wait_ge(blank.sem, 1)
                    sp.dma_start(xt[P - N_META:P, :], meta_tokens).then_inc(x_in.sem, 16)
                else:
                    sp.dma_start(xt[:], x2[bass.ds((t + 1) * P, P), :]).then_inc(x_in.sem, 16)
            if live(t, 1):
                after(sp, h_s, t - 1)
                sp.dma_start(xres[:], x2[bass.ds((t - 1) * P, P), :]).then_inc(xres_in.sem, 16)
            if live(t + 1, 0):
                after(sp, u_s, t + 1)
                sp.dma_start(u_dram[bass.ds((t + 1) * P, P), :], u[:]).then_inc(u_out.sem, 16)
                if live(t + 1, 1):
                    after(sp, u_out, t + 1)
                    after(sp, cv, t, 5)
                    for back in (1, 2):
                        sp.dma_start(um[:, back - 1, :], u_dram[bass.ds((t + 1) * P - back, P), :]).then_inc(um_in.sem, 16)
            if live(t, 1):
                after(sp, h_s, t)
                sp.dma_start(out[bass.ds((t - 1) * P, P), :], h[:]).then_inc(rows_out.sem, 16)
                after(sp, hn_s, t)
                sp.dma_start(hn_dram[bass.ds((t - 1) * P, P), :], hn[:]).then_inc(rows_out.sem, 16)
        schedule(sp, body)
        after(sp, rows_out, TILES)

    @block.tensor
    def _(pe):
        def split_mm(ps, left, right, n, k_range=range(KD)):
            (l_hi, l_lo), (r_hi, r_lo) = left, right
            last = None
            for k in k_range:
                for l, r in ((l_hi, r_hi), (l_hi, r_lo), (l_lo, r_hi)):
                    last = nc.tensor.matmul(ps, l[:, k, :], r[:, k, n:n + ps.shape[1]],
                                            start=(k == k_range[0] and l is l_hi and r is r_hi),
                                            stop=(k == k_range[-1] and l is l_lo))
            return last

        xT, wi, mT, wo = (xT_hi, xT_lo), (wi_hi, wi_lo), (mT_hi, mT_lo), (wo_hi, wo_lo)

        def body(t):
            proj, attn, route = live(t + 1, 0), live(t, 1), live(t - 1, 1)
            full = proj and live(t + 1, 1)
            if proj:
                after(pe, xn_s, t + 1)
                after(pe, h_s, t - 1)
                after(pe, qT_s, t)
                after(pe, c_sb, t)
                for b, ps in enumerate((psE, psF)):
                    for c in range(4):
                        k = 4 * b + c
                        m = nc.tensor.transpose(ps[:, c * P:(c + 1) * P], xn[:, k * P:(k + 1) * P], ident)
                    m.then_inc(xT_ps.sem, 1)
            if attn:
                after(pe, qT_s, t)
                after(pe, kT_s, t)
                after(pe, hT_act, t - 1)
                after(pe, hT_dve, t - 1)
                after(pe, u_s, t)
                after(pe, h_s, t - 1)
                for j, ps in enumerate((psA, psB, psC, psD)):
                    first = isinstance(t, int) and t == 1
                    for i in range(2):
                        hd = 2 * j + i
                        r, c = 64 * (hd // 4), hd % 4
                        m = nc.tensor.matmul(ps[:, i * 256:(i + 1) * 256], qT[r:r + 64, c * P:(c + 1) * P],
                                             kT[r:r + 64, :], start=True, stop=not first)
                        if first:
                            m = nc.tensor.matmul(ps[:, i * 256:(i + 1) * 256], cst[0:1, C_ONE:C_ONE + P],
                                                 pad_mask[0:1, i, :], start=False, stop=True)
                    m.then_inc(s_ps.sem, 1)
            if route:
                after(pe, hT_act, t - 1)
                after(pe, hT_dve, t - 1)
                for k in range(KD):
                    m = nc.tensor.matmul(psH[:, 448:484], hnT[:, k, :], w_rt[:, k, :], start=(k == 0), stop=(k == KD - 1))
                m.then_inc(lg_ps.sem, 1)
            if proj:
                after(pe, xTh, t + 1)
                after(pe, xTl, t + 1)
            if full:
                after(pe, b_sb, t)
                split_mm(psG[:, :], xT, wi, 0).then_inc(pq.sem, 1)
            if attn:
                for j, ps in enumerate((psA, psB, psC, psD)):
                    after(pe, p_sb, t, 2 * j + 2)
                    for i in range(4):
                        hd, c = 2 * j + i // 2, i % 2
                        m = nc.tensor.transpose(ps[:, i * P:(i + 1) * P], prob[:, hd, c * P:(c + 1) * P], ident)
                    m.then_inc(pT_ps.sem, 1)
            if proj:
                after(pe, k_n, t)
                after(pe, v_st, t)
                after(pe, kT_s, t)
                after(pe, rt1, t - 1, 1)
                split_mm(psH[:, 0:256], xT, wi, O_K).then_inc(pkv.sem, 1)
            if attn:
                after(pe, v_cur, t)
                after(pe, pT_act, t)
                after(pe, pT_dve, t)
                for hd in range(HEADS):
                    kv = hd // 4
                    for c in range(2):
                        m = nc.tensor.matmul(psE[:, hd * HD:(hd + 1) * HD], probT[:, hd, c, :],
                                             V[:, c, kv * HD:(kv + 1) * HD], start=(c == 0), stop=(c == 1))
                m.then_inc(o_ps.sem, 1)
            if proj:
                split_mm(psF[:, :], xT, wi, O_C).then_inc(pc.sem, 1)
            if route:
                after(pe, rt1, t - 1)
                after(pe, rt2, t - 2)
                after(pe, counted, t - 2)
                if proj:
                    after(pe, v_st, t + 1)
                    after(pe, k_n, t + 1)
                nc.tensor.matmul(psH[:, 384:416], tri16[:], both16[:], start=True, stop=True)
                nc.tensor.matmul(psH[:, 416:448], one16[:], both16[:], start=True, stop=True).then_inc(cnt_ps.sem, 1)
            if attn:
                for i, (src, ready, ps) in enumerate(((a, a_n, psA), (yc, c_n, psB))):
                    after(pe, ready, t)
                    for c in range(4):
                        m = nc.tensor.transpose(ps[:, c * P:(c + 1) * P], src[:, c * P:(c + 1) * P], ident)
                    m.then_inc(mT_ps.sem, 1)
            if proj:
                if attn:
                    after(pe, pT_act, t)
                split_mm(psC[:, :], xT, wi, O_H).then_inc(ph.sem, 1)
            if attn:
                after(pe, mTh, t)
                after(pe, mTl, t)
                after(pe, pT_dve, t)
                after(pe, a_s, t)
                for n, ps in enumerate((psD, psE)):
                    split_mm(ps[:, :], mT, wo, n * 512).then_inc(h_ps.sem, 1)
            if full:
                after(pe, q_sq, t + 1)
                after(pe, q_n, t + 1)
                split_mm(psG[:, :], xT, wi, O_B).then_inc(pb.sem, 1)
            if full:
                after(pe, c_sb, t + 1)
                for c in range(4):
                    m = nc.tensor.transpose(psF[:, c * P:(c + 1) * P], qn[:, c, :, :].rearrange("p a d -> p (a d)"), ident)
                m.then_inc(qT_ps.sem, 1)
            if proj:
                after(pe, k_n, t + 1)
                after(pe, rt2, t - 1)
                after(pe, counted, t - 1)
                nc.tensor.transpose(psH[:, 256:384], kn[:], ident).then_inc(kT_ps.sem, 1)
            if attn:
                after(pe, hn_s, t)
                for b, ps in enumerate((psA, psB)):
                    for c in range(4):
                        k = 4 * b + c
                        m = nc.tensor.transpose(ps[:, c * P:(c + 1) * P], hn[:, k * P:(k + 1) * P], ident)
                    m.then_inc(hT_ps.sem, 1)
        schedule(pe, body)

    @block.scalar
    def _(act):
        s = nc.scalar

        def rstd(signal, t, ss, ln, r, width):
            s.activation(ln, ss, ACT.Ln, bias=eps, scale=1.0 / width).then_inc(signal.sem, 1)
            after(act, signal, t, 1)
            s.activation(r, ln, ACT.Exp, scale=-0.5).then_inc(signal.sem, 1)

        def body(t):
            proj, attn, route = live(t + 1, 0), live(t, 1), live(t - 1, 1)
            full = proj and live(t + 1, 1)
            if proj:
                after(act, pb, t)
                after(act, ph, t)
                for b, ps in enumerate((psE, psF)):
                    after(act, xT_ps, t + 1, b + 1)
                    s.activation(xT_hi[:, 4 * b:4 * b + 4, :].rearrange("p k c -> p (k c)"), ps[:, :], ACT.Copy,
                                 scale=XS).then_inc(xTh.sem, 1)
            if attn:
                for hd in range(HEADS):
                    if hd % 2 == 0:
                        after(act, n_top, t, hd // 2 + 1)
                    s.activation(prob[:, hd, :], prob[:, hd, :], ACT.Exp, bias=ntop[:, hd:hd + 1],
                                 accum_out=psum_[:, hd:hd + 1]).then_inc(p_sb.sem, 1)
                after(act, sink_ds, t)
                s.activation(sink_e, sink_d, ACT.Exp).then_inc(sink_es.sem, 1)
            if live(t + 2, 0):
                after(act, x_in, t + 2)
                after(act, x_rs, t + 1)
                after(act, xn_s, t + 1)
                s.activation(dump[:], xt[:], ACT.Square, accum_out=ss_x).then_inc(x_sq.sem, 1)
                after(act, x_sq, t + 2)
                rstd(x_rs, t + 2, ss_x, ln1[0], r_x, D)
            if full:
                after(act, pq, t + 1)
                after(act, q_ss, t)
                s.activation(qsq[:], psG[:, :], ACT.Square, scale=inv_in).then_inc(q_sq.sem, 1)
            if attn:
                for b, ps in ((0, psA), (2, psC)):
                    after(act, pT_ps, t, b + 1)
                    after(act, o_ps, t - 1)
                    s.activation(probT[:, 2 * b:2 * b + 2, :, :].rearrange("p a c q -> p (a c q)"), ps[:, :],
                                 ACT.Copy).then_inc(pT_act.sem, 1)
            if route:
                after(act, rt1, t - 1, 3)
                s.activation(rs[:, 20:24], lgb[:, 0:GROUPS], ACT.Exp, bias=rs[:, 1:2],
                             accum_out=rs[:, 2:3]).then_inc(rt_e.sem, 1)
            if full:
                after(act, q_ss, t + 1)
                after(act, q_n, t)
                rstd(q_rs, t + 1, ss_q, ln_q, r_q, HD)
            if proj:
                after(act, pkv, t + 1)
                after(act, k_ss, t)
                s.activation(ksq[:], psH[:, 0:P], ACT.Square, scale=inv_in).then_inc(k_sq.sem, 1)
                after(act, v_cur, t)
                s.activation(vst[:], psH[:, P:2 * P], ACT.Copy, scale=inv_in).then_inc(v_st.sem, 1)
                after(act, k_ss, t + 1)
                after(act, k_n, t)
                rstd(k_rs, t + 1, ss_k, ln_k, r_k, HD)
            if attn:
                after(act, cv, t)
                s.activation(dump[:, 0:CC], yc[:], ACT.Square, accum_out=ss_c).then_inc(c_sq.sem, 1)
                after(act, c_sq, t)
                after(act, c_n, t - 1)
                rstd(c_rs, t, ss_c, ln1[2], r_c, CC)
                after(act, a_s, t)
                s.activation(dump[:, 0:AD], a[:], ACT.Square, accum_out=ss_a).then_inc(a_sq.sem, 1)
                after(act, a_sq, t)
                after(act, a_n, t - 1)
                rstd(a_rs, t, ss_a, ln1[1], r_a, AD)
                after(act, a_rs, t)
                s.activation(a[:], a[:], ACT.Copy, scale=r_a).then_inc(a_n.sem, 1)
            if route:
                after(act, rt1, t - 1, 17)
                s.activation(rs[:, 12:13], rs[:, 11:12], ACT.Exp).then_inc(rt_e.sem, 1)
            if proj:
                after(act, pc, t + 1)
                after(act, u_s, t)
                s.activation(Cs[:], psF[:, :], ACT.Copy, scale=inv_in).then_inc(c_sb.sem, 1)
            if attn:
                after(act, h_ps, t - 1)
                for i, ps in enumerate((psA, psB)):
                    after(act, mT_ps, t, i + 1)
                    s.activation(mT_hi[:, 4 * i:4 * i + 4, :].rearrange("p k c -> p (k c)"), ps[:, :], ACT.Copy,
                                 scale=XS).then_inc(mTh.sem, 1)
                after(act, h_s, t)
                s.activation(dump[:], h[:], ACT.Square, accum_out=ss_h).then_inc(h_sq.sem, 1)
                after(act, h_sq, t)
                after(act, hn_s, t - 1)
                rstd(h_rs, t, ss_h, ln1[3], r_h, D)
            if full:
                after(act, pb, t + 1)
                after(act, cv, t)
                s.activation(Bs[:], psG[:, :], ACT.Copy, scale=inv_in).then_inc(b_sb.sem, 1)
            if attn:
                after(act, hT_ps, t, 1)
                after(act, lg_ps, t - 1)
                s.activation(hnT[:, 0:4, :].rearrange("p k c -> p (k c)"), psA[:, :], ACT.Copy).then_inc(hT_act.sem, 1)
        schedule(act, body)

    @block.gpsimd
    def _(pool):
        g = nc.gpsimd
        g.memset(xt[:], 0.0).then_inc(blank.sem, 1)

        def body(t):
            proj, attn, route = live(t + 1, 0), live(t, 1), live(t - 1, 1)
            if attn:
                after(pool, um_in, t)
                after(pool, u_s, t)
                after(pool, mT_ps, t - 1)
                g.tensor_tensor(yc[:], u[:], w_cv[:, 2, :], ALU.mult).then_inc(cv.sem, 1)
                g.tensor_tensor(um[:, 0, :], um[:, 0, :], w_cv[:, 1, :], ALU.mult).then_inc(cv.sem, 1)
                g.tensor_tensor(um[:, 1, :], um[:, 1, :], w_cv[:, 0, :], ALU.mult).then_inc(cv.sem, 1)
                after(pool, cv, t, 3)
                g.tensor_tensor(yc[:], yc[:], um[:, 0, :], ALU.add).then_inc(cv.sem, 1)
                after(pool, cv, t, 4)
                g.tensor_tensor(yc[:], yc[:], um[:, 1, :], ALU.add).then_inc(cv.sem, 1)
                after(pool, cv, t, 5)
                after(pool, b_sb, t)
                g.tensor_tensor(yc[:], yc[:], Bs[:], ALU.mult).then_inc(cv.sem, 1)
            if live(t + 2, 0):
                after(pool, x_rs, t + 2)
                after(pool, xT_ps, t + 1)
                hold(pool, pool_held)
                g.tensor_scalar(xn[:], xt[:], r_x, None, ALU.mult).then_inc(xn_s.sem, 1)
            if attn:
                after(pool, c_rs, t)
                hold(pool, pool_held)
                g.tensor_scalar(yc[:], yc[:], r_c, None, ALU.mult).then_inc(c_n.sem, 1)
            if proj:
                if live(t + 1, 1):
                    after(pool, o_ps, t)
                    after(pool, v_cur, t)
                    hold(pool, pool_held)
                    g.tensor_copy(V[:, 0, :], V[:, 1, :]).then_inc(v_prev.sem, 1)
                    after(pool, v_prev, t + 1)
                after(pool, v_st, t + 1)
                hold(pool, pool_held)
                g.tensor_copy(V[:, 1, :], vst[:]).then_inc(v_cur.sem, 1)
            if route:
                after(pool, rt2, t - 1)
                hold(pool, pool_held)
                for n in range(2):
                    g.indirect_dma_start(table, bass.IndirectOffsetOnAxis(ap=slot[:, n:n + 1], axis=0),
                                         entry[:, n, :], None, bounds_check=E * CAP - 1).then_inc(listed.sem, 16)
        schedule(pool, body)
        after(pool, listed, TILES)

    @block.vector
    def _(dve):
        v = nc.vector

        def body(t):
            proj, attn, route = live(t + 1, 0), live(t, 1), live(t - 1, 1)
            full = proj and live(t + 1, 1)

            def lo_half(out, ps, hi, signal):
                v.scalar_tensor_tensor(out.rearrange("p k c -> p (k c)"), ps[:, :], XS,
                                       hi.rearrange("p k c -> p (k c)"), ALU.mult, ALU.subtract).then_inc(signal.sem, 1)

            if proj:
                after(dve, pb, t)
                after(dve, ph, t)
                for b, ps in enumerate((psE, psF)):
                    after(dve, xTh, t + 1, b + 1)
                    lo_half(xT_lo[:, 4 * b:4 * b + 4, :], ps, xT_hi[:, 4 * b:4 * b + 4, :], xTl)
            if attn:
                after(dve, pT_ps, t - 1)
                after(dve, sink_es, t - 1)
                after(dve, den_s, t - 1)
                for j, ps in enumerate((psA, psB, psC, psD)):
                    after(dve, s_ps, t, j + 1)
                    hold(dve, dve_held)
                    for i in range(2):
                        hd = 2 * j + i
                        v.tensor_tensor_reduce(prob[:, hd, :], ps[:, i * 256:(i + 1) * 256], bias[:, hd, :], 1.0,
                                               sinks[:, hd:hd + 1], ALU.add, ALU.max,
                                               top[:, hd:hd + 1]).then_inc(s_sb.sem, 1)
                    after(dve, s_sb, t, 2 * j + 2)
                    v.tensor_scalar(ntop[:, 2 * j:2 * j + 2], top[:, 2 * j:2 * j + 2], -1.0, None,
                                    ALU.mult).then_inc(n_top.sem, 1)
                after(dve, n_top, t)
                v.tensor_tensor(sink_d, sinks[:], ntop, ALU.add).then_inc(sink_ds.sem, 1)
            if route:
                n1 = [0]

                def step(ins):
                    n1[0] += 1
                    ins.then_inc(rt1.sem, 1)
                    after(dve, rt1, t - 1, n1[0])

                w4, w32 = cst[:, C_W4:C_W4 + GROUPS], cst[:, C_W32:C_W32 + E]
                gm, ngm, m4, v1, m1, v2, m2 = (rs[:, c:c + 1] for c in (0, 1, 3, 4, 5, 6, 7))
                after(dve, lg_ps, t - 1)
                step(v.tensor_tensor(lgb[:], psH[:, 448:484], b_rt[:], ALU.add))
                step(v.tensor_reduce(gm, lgb[:, 0:GROUPS], AX, ALU.max))
                step(v.tensor_scalar(ngm, gm, -1.0, None, ALU.mult))
                step(v.scalar_tensor_tensor(cand[:, 0:GROUPS], lgb[:, 0:GROUPS], gm, w4, ALU.is_equal, ALU.mult))
                step(v.tensor_reduce(m4, cand[:, 0:GROUPS], AX, ALU.max))
                step(v.tensor_scalar(oh4[:], w4, m4, None, ALU.is_equal))
                step(v.tensor_scalar(pen4[:], oh4[:], -NEG, NEG, ALU.mult, ALU.add))
                step(v.tensor_tensor(lm[:].rearrange("p (g e) -> p g e", g=GROUPS),
                                     lgb[:, GROUPS:].rearrange("p (g e) -> p g e", g=GROUPS),
                                     pen4[:].unsqueeze(2).to_broadcast([P, GROUPS, PER_GROUP]), ALU.add))
                step(v.tensor_reduce(v1, lm[:], AX, ALU.max))
                step(v.scalar_tensor_tensor(cand[:], lm[:], v1, w32, ALU.is_equal, ALU.mult))
                step(v.tensor_reduce(m1, cand[:], AX, ALU.max))
                step(v.tensor_scalar(hot1[:], w32, m1, None, ALU.is_equal))
                step(v.scalar_tensor_tensor(lm[:], hot1[:], -3e38, lm[:], ALU.mult, ALU.add))
                step(v.tensor_reduce(v2, lm[:], AX, ALU.max))
                step(v.scalar_tensor_tensor(cand[:], lm[:], v2, w32, ALU.is_equal, ALU.mult))
                step(v.tensor_reduce(m2, cand[:], AX, ALU.max))
                step(v.tensor_tensor(rs[:, 11:12], v2, v1, ALU.subtract))
                v.tensor_scalar(hot2[:], w32, m2, None, ALU.is_equal).then_inc(hot2_s.sem, 1)
                after(dve, hot2_s, t - 1)
                after(dve, cnt_ps, t - 2)
                step(v.tensor_tensor(both16[:], hot1[:], hot2[:], ALU.add))
            if attn:
                for b, ps in ((1, psB), (3, psD)):
                    after(dve, pT_ps, t, b + 1)
                    after(dve, o_ps, t - 1)
                    v.tensor_copy(probT[:, 2 * b:2 * b + 2, :, :].rearrange("p a c q -> p (a c q)"),
                                  ps[:, :]).then_inc(pT_dve.sem, 1)
                after(dve, sink_es, t)
                after(dve, p_sb, t)
                v.tensor_tensor(den, psum_, sink_e, ALU.add).then_inc(den_s.sem, 1)
                after(dve, den_s, t, 1)
                v.reciprocal(den, den).then_inc(den_s.sem, 1)
            if full:
                after(dve, q_sq, t + 1)
                after(dve, q_rs, t)
                v.tensor_reduce(ss_q, qsq[:].rearrange("p (h d) -> p h d", h=HEADS), AX, ALU.add).then_inc(q_ss.sem, 1)
                after(dve, q_rs, t + 1)
                after(dve, qT_ps, t)
                for kv in range(KV):
                    v.scalar_tensor_tensor(qn[:, :, kv, :],
                                           psG[:, kv * 256:(kv + 1) * 256].rearrange("p (c d) -> p c d", c=4), inv_in,
                                           r_q[:, 4 * kv:4 * kv + 4].unsqueeze(2).to_broadcast([P, 4, HD]),
                                           ALU.mult, ALU.mult).then_inc(q_n.sem, 1)
            if proj:
                after(dve, k_sq, t + 1)
                after(dve, k_rs, t)
                v.tensor_reduce(ss_k, ksq[:].rearrange("p (h d) -> p h d", h=KV), AX, ALU.add).then_inc(k_ss.sem, 1)
            if attn:
                after(dve, o_ps, t)
                after(dve, den_s, t)
                after(dve, mT_ps, t - 1)
                v.tensor_tensor(a[:].rearrange("p (h d) -> p h d", h=HEADS),
                                psE[:, :].rearrange("p (h d) -> p h d", h=HEADS),
                                den.unsqueeze(2).to_broadcast([P, HEADS, HD]), ALU.mult).then_inc(a_s.sem, 1)
            if proj:
                after(dve, k_rs, t + 1)
                after(dve, kT_ps, t)
                v.scalar_tensor_tensor(kn[:].rearrange("p (h d) -> p h d", h=KV),
                                       psH[:, 0:P].rearrange("p (h d) -> p h d", h=KV), inv_in,
                                       r_k.unsqueeze(2).to_broadcast([P, KV, HD]),
                                       ALU.mult, ALU.mult).then_inc(k_n.sem, 1)
            if route:
                n2 = [0]

                def step2(ins):
                    n2[0] += 1
                    ins.then_inc(rt2.sem, 1)
                    after(dve, rt2, t - 1, n2[0])

                gp, ed, one_ed = rs[:, 13:14], rs[:, 12:13], rs[:, 14:15]
                gates = entry[:].bitcast(F32)
                after(dve, listed, t - 2)
                after(dve, rt_e, t - 1)
                step2(v.reciprocal(gp, rs[:, 2:3]))
                step2(v.tensor_scalar(one_ed, ed, 1.0, None, ALU.add))
                step2(v.reciprocal(one_ed, one_ed))
                step2(v.tensor_tensor(gates[:, 0, 1:2], gp, one_ed, ALU.mult))
                step2(v.tensor_tensor(gates[:, 1, 1:2], gates[:, 0, 1:2], ed, ALU.mult))
                after(dve, cnt_ps, t - 1)
                step2(v.tensor_tensor(rank[:], psH[:, 384:416], running[:], ALU.add))
                v.tensor_tensor_reduce(cand[:], hot1[:], rank[:], 1.0, 0.0, ALU.mult, ALU.add, rs[:, 16:17]).then_inc(rt2.sem, 1)
                v.tensor_tensor_reduce(lm[:], hot2[:], rank[:], 1.0, 0.0, ALU.mult, ALU.add, rs[:, 17:18]).then_inc(rt2.sem, 1)
                n2[0] += 2
                after(dve, rt2, t - 1, n2[0])
                v.tensor_tensor(running[:], running[:], psH[:, 416:448], ALU.add).then_inc(counted.sem, 1)
                v.tensor_copy(entry[:, :, 0], tok[:].to_broadcast([P, 2])).then_inc(counted.sem, 1)
                after(dve, counted, t - 1)
                step2(v.tensor_copy(slot[:], rs[:, 16:18]))
                step2(v.tensor_scalar(tok[:], tok[:], float(P), None, ALU.add))
                assert n2[0] == R2
            if attn:
                after(dve, h_ps, t - 1)
                for i, ps in enumerate((psA, psB)):
                    after(dve, mTh, t, i + 1)
                    lo_half(mT_lo[:, 4 * i:4 * i + 4, :], ps, mT_hi[:, 4 * i:4 * i + 4, :], mTl)
            if proj:
                after(dve, ph, t + 1)
                after(dve, c_sb, t + 1)
                after(dve, u_out, t)
                after(dve, cv, t, 1)
                v.scalar_tensor_tensor(u[:], psC[:, :], inv_in, Cs[:], ALU.mult, ALU.mult).then_inc(u_s.sem, 1)
            if attn:
                after(dve, xres_in, t)
                after(dve, rows_out, t - 1)
                for n, ps in enumerate((psD, psE)):
                    after(dve, h_ps, t, n + 1)
                    c = slice(n * 512, (n + 1) * 512)
                    v.scalar_tensor_tensor(h[:, c], ps[:, :], inv_out, xres[:, c], ALU.mult, ALU.add).then_inc(h_s.sem, 1)
                after(dve, h_s, t)
                after(dve, h_rs, t)
                after(dve, hT_ps, t - 1)
                v.scalar_tensor_tensor(hn[:], h[:], r_h, g_ffn[:], ALU.mult, ALU.mult).then_inc(hn_s.sem, 1)
            if full:
                after(dve, qT_ps, t + 1)
                after(dve, s_ps, t)
                v.tensor_copy(qT[:], psF[:, :]).then_inc(qT_s.sem, 1)
                after(dve, kT_s, t)
                v.tensor_copy(kT[:, 0:P], kT[:, P:2 * P]).then_inc(k_prev.sem, 1)
                after(dve, k_prev, t + 1)
            if proj:
                after(dve, kT_ps, t + 1)
                v.tensor_scalar(kT[:, P:2 * P], psH[:, 256:384], g_qk[:, 0:1], None, ALU.mult).then_inc(kT_s.sem, 1)
            if attn:
                after(dve, hT_ps, t, 2)
                after(dve, lg_ps, t - 1)
                v.tensor_copy(hnT[:, 4:8, :].rearrange("p k c -> p (k c)"), psB[:, :]).then_inc(hT_dve.sem, 1)

        schedule(dve, body)
        steps = [0]
        last = sig("last").sem

        def step(ins):
            steps[0] += 1
            ins.then_inc(last, 1)
            dve.wait_ge(last, steps[0])

        nb, ping, pong = hot1, hot2, rank
        counts = slice(0, E)
        step(v.tensor_tensor(nb[:], running[:], cst[:, C_SLOT:C_SLOT + E], ALU.subtract))
        step(v.tensor_scalar(blocks_of[:, counts], nb[:], float(P - 1), None, ALU.add))
        step(v.tensor_scalar(blocks_of[:, E:], blocks_of[:, counts], 7, None, ALU.arith_shift_right))
        step(v.tensor_scalar(blocks_of[:, counts], blocks_of[:, E:], 1, None, ALU.max))
        step(v.tensor_scalar(blocks_of[:, 0:1], blocks_of[:, 0:1], 2, None, ALU.max))
        step(v.tensor_copy(nb[:], blocks_of[:, counts]))
        step(v.tensor_copy(ping[:], nb[:]))
        shift = 1
        while shift < E:
            step(v.tensor_copy(pong[:, 0:shift], ping[:, 0:shift]))
            step(v.tensor_tensor(pong[:, shift:], ping[:, shift:], ping[:, 0:E - shift], ALU.add))
            ping, pong = pong, ping
            shift *= 2
        step(v.tensor_tensor(blocks_of[:, E:], ping[:], nb[:], ALU.subtract))



def experts(nc, ctx, env):
    w_gate, w_up, w_down, out, table, hn_dram, cst, ident, blocks_of = (env[n] for n in (
        "w_gate w_up w_down out table hn_dram cst ident blocks_of").split())
    psA, psB, psC, psD, psE, psF, psG = (env[f"ps{c}"] for c in "ABCDEFG")

    def sb(name, shape, dt=F32):
        return ctx.enter_context(nc.sbuf_tensor(name, shape, dt))

    def sem(name):
        return ctx.enter_context(nc.semaphore(name))

    raw = {n: sb(f"raw_{n}", [P, 8, 512]) for n in ("gate", "up", "down")}
    hi = {n: sb(f"{n}_hi", [P, 8, 512], F32R) for n in raw}
    lo = {n: sb(f"{n}_lo", [P, 8, 512], F32R) for n in raw}
    xg = sb("xg", [P, D])
    gT_hi, gT_lo = sb("gT_hi", [P, KD, P], F32R), sb("gT_lo", [P, KD, P], F32R)
    gated, act_rows = sb("gated", [P, DE]), sb("act_rows", [P, DE])
    aT_hi, aT_lo = sb("aT_hi", [P, KE, P], F32R), sb("aT_lo", [P, KE, P], F32R)
    y = sb("y", [P, D])
    slots, slots_old = sb("slots", [P, 4, 2], I32), sb("slots_old", [P, 3, 2], I32)

    raw_in = {n: sem(f"raw_in_{n}") for n in raw}
    hi_s = {n: sem(f"hi_s_{n}") for n in raw}
    lo_s = {n: sem(f"lo_s_{n}") for n in raw}
    slots_in, moved, shifted, rows_in = sem("slots_in"), sem("moved"), sem("shifted"), sem("rows_in")
    xgT_ps, xgT_hi, xgT_lo = sem("xgT_ps"), sem("xgT_hi"), sem("xgT_lo")
    gate_ps, up_ps, silu_s, act_s = sem("gate_ps"), sem("up_ps"), sem("silu_s"), sem("act_s")
    aT_ps, aT_hi_s, aT_lo_s, y_ps = sem("aT_ps"), sem("aT_hi_s"), sem("aT_lo_s"), sem("y_ps")
    y_act, y_dve, added, cleared = sem("y_act"), sem("y_dve"), sem("added"), sem("cleared")
    held = sem("held")

    w_dram = {
        "gate": lambda e: w_gate[0, bass.ds(e, 1)].rearrange("o (k p) n -> p (o k) n", p=P),
        "up": lambda e: w_up[0, bass.ds(e, 1)].rearrange("o (k p) n -> p (o k) n", p=P),
        "down": lambda e: w_down[0, bass.ds(e, 1)].rearrange("o (k p) n -> p (o k) n", p=P),
    }

    def walk(eng, block, before=None):
        def loads(e):
            n = eng.value_load(blocks_of[0:1, bass.ds(e, 1)], min_val=1, max_val=TILES)
            base = eng.value_load(blocks_of[0:1, bass.ds(e + E, 1)], min_val=0, max_val=3 * TILES)
            return n, base

        n, _ = loads(0)
        block(0, 0, 0, True)
        block(0, 1, 1, False)
        with eng.If(n > 2):
            with eng.Fori(2, n) as i:
                block(0, i, i, False)
        with eng.Fori(1, E) as e:
            n, base = loads(e)
            block(e, 0, base, True)
            with eng.If(n > 1):
                with eng.Fori(1, n) as i:
                    block(e, i, base + i, False)
        n, base = loads(E - 1)
        return base + n

    block = ctx.enter_context(nc.Block())

    @block.sync
    def _(sp):
        def load(e, first=False):
            for n in ("gate", "up", "down"):
                if not first:
                    sp.wait_ge(hi_s[n], 8 * e)
                    sp.wait_ge(lo_s[n], 8 * e)
                dst = raw[n][:] if n != "down" else raw[n][:].rearrange("p (k a) n -> p k (a n)", k=KE)
                sp.dma_start(dst, w_dram[n](e)).then_inc(raw_in[n], 16)
        load(0, True)
        with sp.Fori(1, E) as e:
            load(e)

    @block.gpsimd
    def _(pool):
        g = nc.gpsimd

        def gather():
            pool.indirect_dma_start(xg[:], None, hn_dram, bass.IndirectOffsetOnAxis(ap=slots[:, 0, 0:1], axis=0),
                                    bounds_check=SEQ + P - 1).then_inc(rows_in, 16)

        def scatter(b):
            pool.wait_ge(y_act, b + 1)
            pool.wait_ge(y_dve, b + 1)
            hold(pool, held)
            pool.indirect_dma_start(out, bass.IndirectOffsetOnAxis(ap=slots[:, 3, 0:1], axis=0), y[:], None,
                                    compute_op=ALU.add, bounds_check=SEQ + P - 1).then_inc(added, 16)
            pool.wait_ge(added, 16 * b + 16)
            hold(pool, held)

        def shift(b):
            g.tensor_copy(slots_old[:], slots[:, 0:3, :]).then_inc(moved, 1)
            pool.wait_ge(moved, b + 1)
            hold(pool, held)
            g.tensor_copy(slots[:, 1:4, :], slots_old[:]).then_inc(shifted, 1)
            pool.wait_ge(shifted, b + 1)
            hold(pool, held)

        def block_(e, i, b, first):
            shift(b)
            pool.dma_start(slots[:, 0, :], table[bass.ds(e * CAP + i * P, P), :]).then_inc(slots_in, 16)
            pool.wait_ge(slots_in, 16 * (b + 1))
            if not (isinstance(b, int) and b == 0):
                pool.wait_ge(xgT_ps, 2 * b)
                hold(pool, held)
            gather()
            scatter(b)
            pool.wait_ge(rows_in, 16 * (b + 1))
            hold(pool, held)

        pool.wait_ge(cleared, 3)
        total = walk(pool, block_)
        shift(total)
        pool.wait_ge(xgT_ps, 2 * total)
        hold(pool, held)
        gather()
        scatter(total)
        pool.wait_ge(rows_in, 16 * (total + 1))
        hold(pool, held)
        shift(total + 1)
        scatter(total + 1)
        shift(total + 2)
        scatter(total + 2)

    @block.tensor
    def _(pe):
        def split_mm(ps, l_k, left, right, r_k, fresh, name=None, e=0):
            for n, k in enumerate(l_k):
                if fresh:
                    pe.wait_ge(hi_s[name], e * 8 + r_k[n] + 1)
                    pe.wait_ge(lo_s[name], e * 8 + r_k[n] + 1)
                for j, (l, r) in enumerate(((left[0], right[0]), (left[0], right[1]), (left[1], right[0]))):
                    m = nc.tensor.matmul(ps[:, :], l[:, k, :], r[:, r_k[n], :], start=(n == 0 and j == 0),
                                         stop=(n == len(l_k) - 1 and j == 2))
            return m

        def transpose_rows(b):
            pe.wait_ge(rows_in, 16 * (b + 1))
            for h, ps in enumerate((psC, psD)):
                for c in range(4):
                    m = nc.tensor.transpose(ps[:, c * P:(c + 1) * P], xg[:, (4 * h + c) * P:(4 * h + c + 1) * P], ident)
                m.then_inc(xgT_ps, 1)

        def turn_act(b):
            pe.wait_ge(act_s, b)
            for c in range(KE):
                m = nc.tensor.transpose(psE[:, c * P:(c + 1) * P], act_rows[:, c * P:(c + 1) * P], ident)
            m.then_inc(aT_ps, 1)

        def down(b):
            pe.wait_ge(aT_hi_s, b)
            pe.wait_ge(aT_lo_s, b)
            pe.wait_ge(y_act, b + 2)
            pe.wait_ge(y_dve, b + 2)
            for half, ps in enumerate((psF, psG)):
                split_mm(ps, range(KE), (aT_hi, aT_lo), (hi["down"], lo["down"]), [2 * k + half for k in range(KE)],
                         False).then_inc(y_ps, 1)

        def block_(e, i, b, first):
            static0 = isinstance(b, int) and b == 0
            pe.wait_ge(xgT_hi, 2 * (b + 1))
            pe.wait_ge(xgT_lo, 2 * (b + 1))
            if not static0:
                pe.wait_ge(silu_s, b)
            split_mm(psA, range(KD), (gT_hi, gT_lo), (hi["gate"], lo["gate"]), list(range(KD)), first, "gate", e
                     ).then_inc(gate_ps, 1)
            if not static0:
                turn_act(b)
            split_mm(psB, range(KD), (gT_hi, gT_lo), (hi["up"], lo["up"]), list(range(KD)), first, "up", e
                     ).then_inc(up_ps, 1)
            transpose_rows(b + 1)
            if not static0:
                loaded = 8 * e if first else 8 * (e + 1)
                pe.wait_ge(hi_s["down"], loaded)
                pe.wait_ge(lo_s["down"], loaded)
                down(b)

        pe.sem_inc(y_ps, 4)
        transpose_rows(0)
        total = walk(pe, block_)
        turn_act(total)
        pe.wait_ge(hi_s["down"], 8 * E)
        pe.wait_ge(lo_s["down"], 8 * E)
        down(total)

    def halves(eng, split, copy_y, act_stage, turn, turn_x):
        def block_(e, i, b, first):
            known = isinstance(b, int)
            if first:
                if not (known and b == 0):
                    eng.wait_ge(gate_ps, b)
                split("gate", e)
            if not (known and b < 2):
                copy_y(b)
            if first:
                if not (known and b == 0):
                    eng.wait_ge(up_ps, b)
                split("up", e)
            if not (known and b == 0):
                turn(b)
            act_stage(b)
            turn_x(b + 1)
            if first:
                if not (known and b == 0):
                    eng.wait_ge(y_ps, 2 * b + 4)
                split("down", e)
        turn_x(0)
        total = walk(eng, block_)
        copy_y(total)
        turn(total)
        copy_y(total + 1)

    gate_of = slots[:, 3, 1:2].bitcast(F32)

    @block.scalar
    def _(act):
        s = nc.scalar

        def split(n, e):
            act.wait_ge(raw_in[n], 16 * (e + 1))
            for k in range(8):
                s.activation(hi[n][:, k, :], raw[n][:, k, :], ACT.Copy).then_inc(hi_s[n], 1)

        def copy_y(b):
            act.wait_ge(y_ps, 2 * b + 1)
            act.wait_ge(shifted, b + 2)
            act.wait_ge(added, 16 * b + 16)
            s.activation(y[:, 0:512], psF[:, :], ACT.Copy, scale=gate_of).then_inc(y_act, 1)

        def silu(b):
            act.wait_ge(gate_ps, b + 1)
            if not (isinstance(b, int) and b == 0):
                act.wait_ge(act_s, b)
            s.activation(gated[:], psA[:, :], ACT.Silu).then_inc(silu_s, 1)

        def turn(b):
            act.wait_ge(aT_ps, b)
            act.wait_ge(y_ps, 2 * b + 2)
            s.activation(aT_hi[:].rearrange("p k c -> p (k c)"), psE[:, :], ACT.Copy).then_inc(aT_hi_s, 1)

        def turn_x(b):
            if not (isinstance(b, int) and b == 0):
                act.wait_ge(up_ps, b)
            for h, ps in enumerate((psC, psD)):
                act.wait_ge(xgT_ps, 2 * b + h + 1)
                s.activation(gT_hi[:, 4 * h:4 * h + 4, :].rearrange("p k c -> p (k c)"), ps[:, :],
                             ACT.Copy).then_inc(xgT_hi, 1)

        act.sem_inc(y_act, 3)
        halves(act, split, copy_y, silu, turn, turn_x)

    @block.vector
    def _(dve):
        v = nc.vector

        def split(n, e):
            dve.wait_ge(raw_in[n], 16 * (e + 1))
            for k in range(8):
                dve.wait_ge(hi_s[n], e * 8 + k + 1)
                v.tensor_tensor(lo[n][:, k, :], raw[n][:, k, :], hi[n][:, k, :].bitcast(F32),
                                ALU.subtract).then_inc(lo_s[n], 1)

        def copy_y(b):
            dve.wait_ge(y_ps, 2 * b + 2)
            dve.wait_ge(shifted, b + 2)
            dve.wait_ge(added, 16 * b + 16)
            v.tensor_scalar(y[:, 512:], psG[:, :], gate_of, None, ALU.mult).then_inc(y_dve, 1)

        def product(b):
            dve.wait_ge(up_ps, b + 1)
            dve.wait_ge(silu_s, b + 1)
            if not (isinstance(b, int) and b == 0):
                dve.wait_ge(aT_ps, b)
            v.tensor_tensor(act_rows[:], psB[:, :], gated[:], ALU.mult).then_inc(act_s, 1)

        def turn(b):
            dve.wait_ge(aT_hi_s, b)
            v.tensor_tensor(aT_lo[:].rearrange("p k c -> p (k c)"), psE[:, :],
                            aT_hi[:].rearrange("p k c -> p (k c)").bitcast(F32), ALU.subtract).then_inc(aT_lo_s, 1)

        def turn_x(b):
            for h, ps in enumerate((psC, psD)):
                dve.wait_ge(xgT_hi, 2 * b + h + 1)
                v.tensor_tensor(gT_lo[:, 4 * h:4 * h + 4, :].rearrange("p k c -> p (k c)"), ps[:, :],
                                gT_hi[:, 4 * h:4 * h + 4, :].rearrange("p k c -> p (k c)").bitcast(F32),
                                ALU.subtract).then_inc(xgT_lo, 1)

        v.memset(y[:], 0.0).then_inc(cleared, 1)
        v.memset(slots[:], 0).then_inc(cleared, 1)
        dve.wait_ge(cleared, 2)
        v.tensor_copy(slots[:, :, 0], cst[:, C_JUNK:C_JUNK + 1].to_broadcast([P, 4])).then_inc(cleared, 1)
        dve.sem_inc(y_dve, 3)
        halves(dve, split, copy_y, product, turn, turn_x)


_INS = ['x', 'meta_tokens', 'rel_bias', 'mix_norm_g', 'w_in', 'q_norm_g', 'k_norm_g', 'attn_sinks', 'conv_w',
        'attn_out_norm_g', 'conv_out_norm_g', 'w_out', 'ffn_norm_g', 'w_group_router', 'b_group_router',
        'w_expert_router', 'b_expert_router', 'w_gate', 'w_up', 'w_down']


def kernel(**inputs):
    import concourse.bacc as bacc
    from concourse.bass_utils import run_bass_kernel_spmd

    nc = bacc.Bacc("TRN2", target_bir_lowering=False, num_devices=1)
    arrays, args = {}, []
    for name, a in [(n, inputs[n]) for n in _INS] + list(zip(("consts", "onehot"), constants())):
        a = np.ascontiguousarray(a)
        arrays[f"in_{name}"] = a
        args.append(nc.dram_tensor(f"in_{name}", a.shape, mybir.dt.from_np(a.dtype), kind="ExternalInput").ap())
    out = nc.dram_tensor("out_rows", (SEQ + P, D), F32, kind="ExternalOutput").ap()
    build(nc, *args, out)
    r = run_bass_kernel_spmd(nc, [arrays], core_ids=[0])
    return r.results[0]["out_rows"][:SEQ].reshape(1, SEQ, D)
```

```python
import math
from contextlib import ExitStack

import numpy as np

import concourse.bass as bass
from concourse import mybir

ALU = mybir.AluOpType
ACT = mybir.ActivationFunctionType
F32 = mybir.dt.float32
F32R = mybir.dt.float32r
F16 = mybir.dt.float16
BF16 = mybir.dt.bfloat16
I32 = mybir.dt.int32
AX = mybir.AxisListType.X
RMAX = bass.bass_isa.ReduceOp.max

P = 128
D = 1024
KD = D // P
SEQ = 4096
TILES = SEQ // P
N_META = 16
HEADS, KV, HD = 8, 2, 64
AD = HEADS * HD
CC = 512
IN = 2304
O_K, O_B, O_C, O_H = 512, 768, 1280, 1792
BUCKETS = 32
GROUPS, PER_GROUP, E = 4, 8, 32
DE = 512
KE = DE // P
CAP = SEQ
EPS = 1e-6
NEG = -1e30
XS = 256.0
PS = 2.0 ** 14
BW = 384

C_ID, C_TRI, C_ONE, C_W32, C_SLOT, C_W4, C_TOK, C_JUNK, C_EPS = 0, 128, 256, 384, 416, 448, 452, 453, 454
CW = 456


def constants():
    c = np.zeros((P, CW), np.float32)
    c[:, C_ID:C_ID + P] = np.eye(P)
    c[:, C_TRI:C_TRI + P] = np.triu(np.ones((P, P)), 1)
    c[:, C_ONE:C_ONE + P] = 1
    c[:, C_W32:C_W32 + E] = np.arange(E, 0, -1)
    c[:, C_SLOT:C_SLOT + E] = np.arange(E) * CAP
    c[:, C_W4:C_W4 + GROUPS] = np.arange(GROUPS, 0, -1)
    c[:, C_TOK] = np.arange(P)
    c[:, C_JUNK] = SEQ + np.arange(P)
    c[:, C_EPS] = EPS
    dist = 2 * P - 1 - np.arange(BW)
    half = BUCKETS // 2
    n = np.maximum(dist, 1).astype(np.float32)
    large = half + (np.log(n / half) / np.float32(math.log(P / half)) * (BUCKETS - half)).astype(np.int32)
    bucket = np.where(dist < half, np.maximum(dist, 0), np.minimum(large, BUCKETS - 1))
    hot = np.zeros((BUCKETS + 1, BW), np.float32)
    hot[bucket, np.arange(BW)] = 1
    hot[BUCKETS] = np.where((dist >= 0) & (dist < P), 0, NEG)
    return c, hot


class Weights:

    def __init__(self, slots, n, cut):
        self.slots, self.n, self.cut = slots, n, cut

    def raw(self, k, lo=0, hi=None):
        return self.slots[:, k + 1, :].bitcast(F32)[:, lo:self.n if hi is None else hi]

    def cols(self, part):
        return (0, self.cut) if part == 0 else (self.cut, self.n)

    def half(self, which, k, c0, width):
        lo, hi = self.cols(int(c0 >= self.cut))
        at = 2 * lo + which * (hi - lo) + c0 - lo
        return self.slots[:, k, at:at + width]

    def spare(self, n):
        return self.slots[:, KD, :].bitcast(F32)[:, 0:n]


class Signal:

    def __init__(self, sem, per=1, first=1):
        self.sem, self.per, self.first = sem, per, first

    def at(self, t, part=None):
        part = self.per if part is None else part
        if isinstance(t, int):
            return self.per * (t - self.first) + part
        return t * self.per + (part - self.per * self.first)


def after(eng, signal, t, part=None):
    value = signal.at(t, part)
    if not isinstance(value, int) or value > 0:
        eng.wait_ge(signal.sem, value)


def hold(eng, passed):
    eng.sem_inc(passed, 1)


def build(nc, x, meta_tokens, rel_bias, mix_norm_g, w_in, q_norm_g, k_norm_g, attn_sinks, conv_w,
          attn_out_norm_g, conv_out_norm_g, w_out, ffn_norm_g, w_group_router, b_group_router,
          w_expert_router, b_expert_router, w_gate, w_up, w_down, consts, onehot, out):
    x2 = x.rearrange("b s d -> (b s) d")
    table = nc.dram_tensor("slot_table", [E * CAP, 2], I32).ap()
    hn_dram = nc.dram_tensor("hn_rows", [SEQ + P, D], F32).ap()
    u_dram = nc.dram_tensor("u_rows", [(TILES + 1) * P, CC], F32).ap()
    band_dram = nc.dram_tensor("band_rows", [P, HEADS * BW], F32).ap()

    def bcast(a, n, offset=0):
        return bass.AP(a.tensor, a.offset + offset, [[0, P], [1, n]])

    with ExitStack() as keep:
        def ksb(name, shape, dt):
            return keep.enter_context(nc.sbuf_tensor(name, shape, dt))

        cst = ksb("cst", [P, CW], F32)
        ident = cst[:, C_ID:C_ID + P]
        blocks_of = ksb("blocks_of", [P, 2 * E], I32)
        wi_all = ksb("wi_all", [P, KD + 1, 2 * IN], F16)
        wi_flat = wi_all[:].rearrange("p s c -> p (s c)").bitcast(F32)
        raw = {n: wi_flat[:, j * 4096:(j + 1) * 4096].rearrange("p (k n) -> p k n", k=8)
               for j, n in enumerate(("gate", "up", "down"))}
        raw_in = {n: keep.enter_context(nc.semaphore(f"raw_in_{n}")) for n in raw}

        def load_expert(sp, n, e):
            w = {"gate": w_gate, "up": w_up, "down": w_down}[n]
            dst = raw[n] if n != "down" else raw[n].rearrange("p (k a) n -> p k (a n)", k=KE)
            sp.dma_start(dst, w[0, bass.ds(e, 1)].rearrange("o (k p) n -> p (o k) n", p=P)).then_inc(raw_in[n], 16)

        psA, psB, psC, psD, psE, psF, psG, psH = (
            keep.enter_context(nc.psum_tensor(f"ps{c}", [P, 512], F32)) for c in "ABCDEFGH")
        with ExitStack() as ctx:
            mixer(nc, ctx, locals())
        with ExitStack() as ctx:
            experts(nc, ctx, locals())


def mixer(nc, ctx, env):
    (x2, meta_tokens, rel_bias, mix_norm_g, w_in, q_norm_g, k_norm_g, attn_sinks, conv_w,
     attn_out_norm_g, conv_out_norm_g, w_out, ffn_norm_g, w_group_router, b_group_router,
     w_expert_router, b_expert_router, consts, onehot, out, table, hn_dram, u_dram, band_dram, bcast,
     cst, ident, blocks_of, wi_all, load_expert, raw) = (env[n] for n in (
         "x2 meta_tokens rel_bias mix_norm_g w_in q_norm_g k_norm_g attn_sinks conv_w attn_out_norm_g "
         "conv_out_norm_g w_out ffn_norm_g w_group_router b_group_router w_expert_router b_expert_router "
         "consts onehot out table hn_dram u_dram band_dram bcast cst ident blocks_of wi_all load_expert raw").split())
    psA, psB, psC, psD, psE, psF, psG, psH = (env[f"ps{c}"] for c in "ABCDEFGH")

    def sb(name, shape, dt=F32):
        return ctx.enter_context(nc.sbuf_tensor(name, shape, dt))

    def sig(name, per=1, first=1):
        return Signal(ctx.enter_context(nc.semaphore(name)), per, first)

    wo_all = sb("wo_all", [P, KD + 1, 2 * D], F16)
    w_in_split, w_out_split = Weights(wi_all, IN, O_C), Weights(wo_all, D, 512)
    w_rt = sb("w_rt", [P, KD, GROUPS + E])
    RT = GROUPS + E
    b_rt, w_rt16 = sb("b_rt", [P, RT]), sb("w_rt16", [P, KD, 2, RT], F16)
    rt_stat = sb("rt_stat", [P, 8])
    tri16, one16 = sb("tri16", [P, P], F16), sb("one16", [P, P], F16)
    g_ffn = sb("g_ffn", [P, D])
    w_cv = sb("w_cv", [P, 3, CC])
    bias = sb("bias", [P, HEADS, 2 * P])
    sinks = sb("sinks", [P, HEADS])
    g_mix, g_out = sb("g_mix", [P, KD]), sb("g_out", [P, KD])
    g_qk = sb("g_qk", [P, 2])
    scale_w = sb("scale_w", [P, 8])
    inv_in, inv_out = scale_w[:, 4:5], scale_w[:, 5:6]
    xt, xres = sb("xt", [P, D]), sb("xres", [P, D])
    xT_hi, xT_lo = sb("xT_hi", [P, KD, P], F16), sb("xT_lo", [P, KD, P], F16)
    dump = sb("dump", [P, D], BF16)
    stat = sb("stat", [P, 64])
    qsq, ksq = sb("qsq", [P, AD]), sb("ksq", [P, KV * HD])
    qn, q2 = qsq, sb("q2", [P, HEADS, 2, HD], F32R)
    kn = sb("kn", [P, KV, 2, HD])
    qT, kT = sb("qT", [P, HEADS * P], F32R), sb("kT", [P, 2, KV, 2 * P], F32R)
    vst, V = sb("vst", [P, KV, 2, HD], F16), sb("V", [P, 2, KV, 2, HD], F16)
    Cs, Bs, u = sb("Cs", [P, CC]), sb("Bs", [P, CC]), sb("u", [P, CC])
    um, yc = sb("um", [P, 2, CC]), sb("yc", [P, CC])
    prob = sb("prob", [P, HEADS, 2 * P])
    both_probT = w_in_split.spare(HEADS * 2 * P).bitcast(F16).rearrange("p (a h c q) -> p a h c q", a=2, h=HEADS, c=2)
    probT_hi, probT_lo = both_probT[:, 0], both_probT[:, 1]
    a = sb("a", [P, AD])
    mT_hi, mT_lo = sb("mT_hi", [P, KD, P], F16), sb("mT_lo", [P, KD, P], F16)
    h, hn = sb("h", [P, D]), sb("hn", [P, D])
    both_hnT = w_out_split.spare(KD * P).bitcast(F16).rearrange("p (a k c) -> p a k c", a=2, k=KD)
    hnT_hi, hnT_lo = both_hnT[:, 0], both_hnT[:, 1]
    lgb, lm, cand = sb("lgb", [P, GROUPS + E]), sb("lm", [P, E]), sb("cand", [P, E])
    oh4, pen4 = sb("oh4", [P, GROUPS]), sb("pen4", [P, GROUPS])
    hot1, hot2, rank = sb("hot1", [P, E]), sb("hot2", [P, E]), sb("rank", [P, E])
    both16 = sb("both16", [P, E], F16)
    running = sb("running", [P, E])
    rs = sb("rs", [P, 24])
    tok = sb("tok", [P, 1])
    slot = sb("slot", [P, 2], I32)
    entry = sb("entry", [P, 2, 2], I32)
    ss_x, r_x, ss_a, r_a, ss_c, r_c, ss_h, r_h = (stat[:, n:n + 1] for n in range(8))
    ln1 = [stat[:, 8 + n:9 + n] for n in range(4)]
    ss_q, ln_q, r_q = stat[:, 12:20], stat[:, 20:28], stat[:, 28:36]
    ss_k, ln_k, r_k = stat[:, 36:38], stat[:, 38:40], stat[:, 40:42]
    soft = sb("soft", [P, 48])
    top, ntop, psum_, sink_d, sink_e, den = (soft[:, 8 * n:8 * n + 8] for n in range(6))
    eps = cst[:, C_EPS:C_EPS + 1]
    v_stat = sb("v_stat", [P, 4])
    v_max, v_root, v_scale, inv_v = (v_stat[:, n:n + 1] for n in range(4))
    hn_scale, inv_rt = rt_stat[:, 4:5], rt_stat[:, 7:8]
    w_sq = h[:].rearrange("p (k c) -> p k c", k=KD)
    O_V = O_K + KV * HD

    x_in, x_rs, xn_s = sig("x_in", 16, 0), sig("x_rs", 3, 0), sig("xn_s", 1, 0)
    blank = sig("blank", 1, 0)
    xT_ps, xTh, xTl = sig("xT_ps", 2, 0), sig("xTh", 2, 0), sig("xTl", 2, 0)
    pq, pkv, pc, ph, pb = sig("pq"), sig("pkv", 1, 0), sig("pc", 1, 0), sig("ph", 1, 0), sig("pb")
    q_sq, q_ss, q_rs, q_n = sig("q_sq"), sig("q_ss"), sig("q_rs", 2), sig("q_n")
    q_hi, q_lo, kT_hi = sig("q_hi"), sig("q_lo"), sig("kT_hi", 1, 0)
    k_sq, k_ss, k_rs, k_n = sig("k_sq", 1, 0), sig("k_ss", 1, 0), sig("k_rs", 2, 0), sig("k_n", 2, 0)
    v_sq, v_cols, v_bound, v_rooted, v_scaled = (sig(n).sem for n in "v_sq v_cols v_bound v_rooted v_scaled".split())
    v_hi, v_st, v_prev, v_cur = sig("v_hi", 1, 0), sig("v_st", 1, 0), sig("v_prev"), sig("v_cur", 1, 0)
    qT_ps, kT_ps, qT_act, qT_dve, k_prev, kT_s = (
        sig("qT_ps", 2), sig("kT_ps", 1, 0), sig("qT_act"), sig("qT_dve"), sig("k_prev"), sig("kT_s", 1, 0))
    c_sb, u_s, u_out, um_in, b_sb = (
        sig("c_sb", 1, 0), sig("u_s", 1, 0), sig("u_out", 16, 0), sig("um_in", 32), sig("b_sb"))
    s_ps, s_sb, n_top, p_sb, sink_ds, sink_es = (
        sig("s_ps", 4), sig("s_sb", 8), sig("n_top", 4), sig("p_sb", 8), sig("sink_ds"), sig("sink_es"))
    pT_ps, pT_act, pT_dve, den_s = sig("pT_ps", 4), sig("pT_act", 4), sig("pT_dve", 4), sig("den_s", 3)
    o_ps, a_s, o_lo, a_rs, a_n = sig("o_ps"), sig("a_s", 3), sig("o_lo", 2), sig("a_rs", 3), sig("a_n")
    cv, c_rs, c_n = sig("cv", 6), sig("c_rs", 3), sig("c_n")
    mT_ps, mTh, mTl = sig("mT_ps", 2), sig("mTh", 2), sig("mTl", 2)
    xres_in, h_ps, h_s, h_rs, hn_s = (
        sig("xres_in", 16), sig("h_ps", 2), sig("h_s", 2), sig("h_rs", 3), sig("hn_s"))
    rows_out = sig("rows_out", 32)
    hT_ps, hT_act, hT_dve = sig("hT_ps", 2), sig("hT_act", 2), sig("hT_dve", 2)
    lg_ps, cnt_ps = sig("lg_ps"), sig("cnt_ps")
    R1, R2 = 19, 10
    rt1, rt2, rt_e = sig("rt1", R1), sig("rt2", R2), sig("rt_e", 2)
    listed = sig("listed", 32)
    dve_held, pool_held = sig("dve_held").sem, sig("pool_held").sem
    hot2_s, counted = sig("hot2_s"), sig("counted", 2)
    (small_in, g_in, cst_in, hot_in, dve_step, pool_step, spread, band_ps, band_sb, band_out, band_in, filled,
     zeroed) = (sig(n).sem for n in "small_in g_in cst_in hot_in dve_step pool_step spread band_ps band_sb "
                "band_out band_in filled zeroed".split())
    w_chunk = {n: [sig(f"w_{n}_{k}").sem for k in range(KD)] for n in ("in", "out")}
    l1_done, bound, all_bound, scaled, hi_done, lo_done = (
        {n: sig(f"{what}_{n}").sem for n in ("in", "out")} for what in
        ("l1_done", "bound", "all_bound", "scaled", "hi_done", "lo_done"))
    splits = {"in": w_in_split, "out": w_out_split}
    g_of = {"in": g_mix, "out": g_out}
    which_of = {"in": 0, "out": 1}
    FIRST_CHUNKS, LAST_CHUNKS = range(KD // 2), range(KD // 2, KD)
    l1 = sb("l1", [P, 2, 2 * KD])
    sI = sb("sI", [P, 8], I32)
    hot, rb = h[0:BUCKETS + 1, 0:BW], h[0:BUCKETS + 1, 512:520]
    rbx, gk = (a, Cs), qsq
    pad_mask = hn[0:1, 2 * BW:2 * BW + 2 * P]
    band_places = [(prob[:].rearrange("p h c -> p (h c)"), 0, 5), (hn, 5, 2), (Bs, 7, 1)]
    banks = (psA, psB, psC, psD, psE, psF, psG, psH)

    def schedule(eng, body):
        for t in range(-2, 3):
            body(t)
        with eng.Fori(3, TILES - 1) as t:
            body(t)
        for t in range(TILES - 1, TILES + 2):
            body(t)

    def live(t, lo, hi=TILES):
        return not isinstance(t, int) or lo <= t <= hi

    block = ctx.enter_context(nc.Block())

    @block.sync
    def _(sp):
        def load_weights(n, w):
            for k in range(KD):
                sp.dma_start(splits[n].raw(k), w[0, k * P:(k + 1) * P, :]).then_inc(w_chunk[n][k], 16)

        def load_gains():
            sp.dma_start(g_mix[:], mix_norm_g.rearrange("o (k p) -> p (o k)", p=P), allow_slow_non_contiguous=True).then_inc(g_in, 16)
            sp.dma_start(g_out[:, 0:4], attn_out_norm_g.rearrange("o (k p) -> p (o k)", p=P), allow_slow_non_contiguous=True).then_inc(g_in, 16)
            sp.dma_start(g_out[:, 4:8], conv_out_norm_g.rearrange("o (k p) -> p (o k)", p=P), allow_slow_non_contiguous=True).then_inc(g_in, 16)
            for half in range(2):
                sp.dma_start(gk[64 * half:64 * half + 64, 0:1], q_norm_g.rearrange("o d -> d o"), allow_slow_non_contiguous=True).then_inc(g_in, 16)
                sp.dma_start(gk[64 * half:64 * half + 64, 1:2], k_norm_g.rearrange("o d -> d o"), allow_slow_non_contiguous=True).then_inc(g_in, 16)

        def load_small():
            sp.dma_start(sinks[:], bcast(attn_sinks, HEADS)).then_inc(small_in, 16)
            sp.dma_start(b_rt[:, 0:GROUPS], bcast(b_group_router, GROUPS)).then_inc(small_in, 16)
            sp.dma_start(b_rt[:, GROUPS:], bcast(b_expert_router, E)).then_inc(small_in, 16)
            sp.dma_start(g_ffn[:], bcast(ffn_norm_g, D)).then_inc(small_in, 16)
            sp.dma_start(w_cv[:].rearrange("p a c -> p (a c)"), bcast(conv_w, 3 * CC)).then_inc(small_in, 16)
            for k in range(KD):
                sp.dma_start(w_rt[:, k, 0:GROUPS], w_group_router[0, k * P:(k + 1) * P, :]).then_inc(small_in, 16)
                sp.dma_start(w_rt[:, k, GROUPS:], w_expert_router[0, k * P:(k + 1) * P].rearrange(
                    "p g e -> p (g e)")).then_inc(small_in, 16)

        sp.dma_start(cst[:], consts).then_inc(cst_in, 16)
        sp.dma_start(hot, onehot).then_inc(hot_in, 16)
        sp.dma_start(rb[0:BUCKETS, :], rel_bias).then_inc(hot_in, 16)

        def body(t):
            first = isinstance(t, int)
            if first and t == TILES:
                after(sp, pb, TILES)
                for n in raw:
                    load_expert(sp, n, 0)
            if live(t + 2, 0):
                after(sp, xT_ps, t + 1)
                if isinstance(t, int) and t == -2:
                    sp.wait_ge(blank.sem, 1)
                    sp.dma_start(xt[P - N_META:P, :], meta_tokens).then_inc(x_in.sem, 16)
                else:
                    sp.dma_start(xt[:], x2[bass.ds((t + 1) * P, P), :]).then_inc(x_in.sem, 16)
            if first and t == -2:
                load_weights("in", w_in)
                load_gains()
            if first and t == -1:
                load_weights("out", w_out)
                load_small()
            if first and t == 1:
                sp.wait_ge(filled, 32)
            if live(t, 1):
                after(sp, h_s, t - 1)
                sp.dma_start(xres[:], x2[bass.ds((t - 1) * P, P), :]).then_inc(xres_in.sem, 16)
            if live(t + 1, 0):
                after(sp, u_s, t + 1)
                sp.dma_start(u_dram[bass.ds((t + 1) * P, P), :], u[:]).then_inc(u_out.sem, 16)
                if live(t + 1, 1):
                    after(sp, u_out, t + 1)
                    after(sp, cv, t, 5)
                    for back in (1, 2):
                        sp.dma_start(um[:, back - 1, :], u_dram[bass.ds((t + 1) * P - back, P), :]).then_inc(um_in.sem, 16)
            if live(t, 1):
                after(sp, h_s, t)
                sp.dma_start(out[bass.ds((t - 1) * P, P), :], h[:]).then_inc(rows_out.sem, 16)
                after(sp, hn_s, t)
                sp.dma_start(hn_dram[bass.ds((t - 1) * P, P), :], hn[:]).then_inc(rows_out.sem, 16)
        schedule(sp, body)
        after(sp, rows_out, TILES)

    @block.tensor
    def _(pe):
        def split_mm(ps, left, name, n, fresh=False, chunks=range(KD)):
            weights, width = splits[name], ps.shape[1]
            for k in chunks:
                if fresh:
                    part = 2 * k + 1 + int(n >= weights.cut)
                    pe.wait_ge(hi_done[name], part)
                    pe.wait_ge(lo_done[name], part)
                for j, (l, r) in enumerate(((0, 0), (0, 1), (1, 0))):
                    m = nc.tensor.matmul(ps, left[l][:, k, :], weights.half(r, k, n, width),
                                         start=(k == 0 and j == 0), stop=(k == KD - 1 and j == 2))
            return m

        def first_projection():
            for k in range(KD):
                for signal, ps, n in ((pkv, psH[:, 0:256], O_K), (pc, psF[:, :], O_C), (ph, psC[:, :], O_H)):
                    m = split_mm(ps, xT, "in", n, True, (k,))
                    if k == KD - 1:
                        m.then_inc(signal.sem, 1)

        pe.wait_ge(hot_in, 32)
        for head in range(HEADS):
            pe.wait_ge(spread, 2 + head // 4)
            nc.tensor.matmul(banks[head][:, 0:BW], rbx[head // 4][0:BUCKETS + 1, head % 4 * P:(head % 4 + 1) * P], hot,
                             start=True, stop=True).then_inc(band_ps, 1)
        pe.wait_ge(cst_in, 16)
        xT, mT = (xT_hi, xT_lo), (mT_hi, mT_lo)

        def body(t):
            proj, attn, route = live(t + 1, 0), live(t, 1), live(t - 1, 1)
            full = proj and live(t + 1, 1)
            new_in, new_out = isinstance(t, int) and t == -1, isinstance(t, int) and t == 1
            if proj:
                if new_in:
                    pe.wait_ge(band_sb, HEADS)
                after(pe, xn_s, t + 1)
                after(pe, h_s, t - 1)
                after(pe, qT_act, t)
                after(pe, c_sb, t)
                for b, ps in enumerate((psE, psF)):
                    for c in range(4):
                        k = 4 * b + c
                        m = nc.tensor.transpose(ps[:, c * P:(c + 1) * P], xt[:, k * P:(k + 1) * P], ident)
                    m.then_inc(xT_ps.sem, 1)
            if attn:
                after(pe, qT_act, t)
                after(pe, kT_s, t)
                for j, ps in enumerate((psA, psB, psC, psD)):
                    first = isinstance(t, int) and t == 1
                    if j == 1:
                        after(pe, qT_dve, t)
                    if j >= 2:
                        after(pe, hT_dve, t - 1, j - 1)
                    for i in range(2):
                        hd = 2 * j + i
                        for half in range(2):
                            m = nc.tensor.matmul(ps[:, i * 256:(i + 1) * 256], qT[:, hd * P:(hd + 1) * P],
                                                 kT[:, half, hd // 4, :], start=(half == 0), stop=(half == 1 and not first))
                        if first:
                            m = nc.tensor.matmul(ps[:, i * 256:(i + 1) * 256], cst[0:1, C_ONE:C_ONE + P],
                                                 pad_mask, start=False, stop=True)
                    m.then_inc(s_ps.sem, 1)
            if route:
                after(pe, hT_dve, t - 1)
                for k in range(KD):
                    for half in ((0, 1) if k < KD - 1 else (1, 0)):
                        m = nc.tensor.matmul(psH[:, 256:256 + (2 - half) * RT], both_hnT[:, half, k, :],
                                             w_rt16[:, k, 0:2 - half, :].rearrange("p a n -> p (a n)"),
                                             start=(k == 0 and half == 0), stop=(k == KD - 1 and half == 0))
                m.then_inc(lg_ps.sem, 1)
            if full:
                after(pe, b_sb, t)
                after(pe, xTl, t + 1, 1)
                split_mm(psG[:, :], xT, "in", 0, False, range(KD // 2))
            if proj:
                after(pe, xTl, t + 1)
            if full:
                split_mm(psG[:, :], xT, "in", 0, False, range(KD // 2, KD)).then_inc(pq.sem, 1)
            if attn:
                for j, ps in enumerate((psA, psB, psC, psD)):
                    after(pe, p_sb, t, 2 * j + 2)
                    for i in range(4):
                        hd, c = 2 * j + i // 2, i % 2
                        m = nc.tensor.transpose(ps[:, i * P:(i + 1) * P], prob[:, hd, c * P:(c + 1) * P], ident)
                    m.then_inc(pT_ps.sem, 1)
            if proj:
                after(pe, k_n, t)
                after(pe, v_st, t)
                after(pe, kT_s, t)
                after(pe, rt1, t - 1, 2)
                if new_in:
                    first_projection()
                else:
                    split_mm(psH[:, 0:256], xT, "in", O_K).then_inc(pkv.sem, 1)
            if new_in:
                for k in range(KD):
                    pe.wait_ge(v_sq, k + 1)
                    m = nc.tensor.matmul(psG[:, 0:P], cst[:, C_ONE:C_ONE + P], w_sq[:, k, :], start=(k == 0), stop=(k == KD - 1))
                m.then_inc(v_cols, 1)
            if attn:
                after(pe, v_cur, t)
                for hd in range(HEADS):
                    after(pe, pT_dve, t, hd // 2 + 1)
                    kv, ps, at = hd // 4, (psE, psA)[hd // 4], hd % 4 * P
                    for c, half in ((0, 0), (0, 1), (1, 1), (1, 0)):
                        m = nc.tensor.matmul(ps[:, at:at + (P, HD)[half]], both_probT[:, half, hd, c, :],
                                             V[:, c, kv, 0:2 - half, :].rearrange("p a d -> p (a d)"),
                                             start=(c == 0 and half == 0), stop=(c == 1 and half == 0))
                m.then_inc(o_ps.sem, 1)
            if full:
                split_mm(psF[:, :], xT, "in", O_C).then_inc(pc.sem, 1)
            if full:
                if attn:
                    after(pe, pT_dve, t)
                split_mm(psC[:, :], xT, "in", O_H, False, range(3))
            if attn:
                for i, (src, ready, ps) in enumerate(((a, a_n, psA), (yc, c_n, psB))):
                    after(pe, ready, t)
                    for c in range(4):
                        m = nc.tensor.transpose(ps[:, c * P:(c + 1) * P], src[:, c * P:(c + 1) * P], ident)
                    m.then_inc(mT_ps.sem, 1)
            if full:
                split_mm(psC[:, :], xT, "in", O_H, False, range(3, KD)).then_inc(ph.sem, 1)
            if attn:
                after(pe, mTh, t)
                after(pe, mTl, t)
                after(pe, pT_dve, t)
                after(pe, a_s, t)
                split_mm(psD[:, :], mT, "out", 0, new_out).then_inc(h_ps.sem, 1)
            if route:
                after(pe, rt1, t - 1)
                after(pe, rt2, t - 2)
                after(pe, counted, t - 2)
                if proj:
                    after(pe, v_st, t + 1)
                    after(pe, k_n, t + 1)
                nc.tensor.matmul(psH[:, 384:416], tri16[:], both16[:], start=True, stop=True)
                nc.tensor.matmul(psH[:, 416:448], one16[:], both16[:], start=True, stop=True).then_inc(cnt_ps.sem, 1)
            if attn:
                split_mm(psE[:, :], mT, "out", 512, new_out).then_inc(h_ps.sem, 1)
            if full:
                after(pe, q_sq, t + 1)
                after(pe, q_n, t + 1)
                split_mm(psG[:, :], xT, "in", O_B).then_inc(pb.sem, 1)
            if proj:
                after(pe, k_n, t + 1)
                after(pe, v_st, t + 1)
                after(pe, rt2, t - 1)
                after(pe, counted, t - 1)
                for kv in range(KV):
                    m = nc.tensor.transpose(psH[:, kv * P:(kv + 1) * P], kn[:, kv, :, :].rearrange("p a d -> p (a d)"), ident)
                m.then_inc(kT_ps.sem, 1)
            if full:
                after(pe, c_sb, t + 1)
                after(pe, q_hi, t + 1)
                after(pe, q_lo, t + 1)
                if attn:
                    after(pe, mTl, t)
                for b, ps in enumerate((psF, psB)):
                    for c in range(4):
                        m = nc.tensor.transpose(ps[:, c * P:(c + 1) * P],
                                                q2[:, 4 * b + c, :, :].rearrange("p a d -> p (a d)").bitcast(F32), ident)
                    m.then_inc(qT_ps.sem, 1)
            if attn:
                after(pe, hn_s, t)
                if proj:
                    after(pe, u_s, t + 1)
                for b, ps in enumerate((psC, psD)):
                    for c in range(4):
                        k = 4 * b + c
                        m = nc.tensor.transpose(ps[:, c * P:(c + 1) * P], hn[:, k * P:(k + 1) * P], ident)
                    m.then_inc(hT_ps.sem, 1)
        schedule(pe, body)

    @block.scalar
    def _(act):
        s = nc.scalar

        def rstd(signal, t, ss, ln, r, width):
            s.activation(ln, ss, ACT.Ln, bias=eps, scale=1.0 / width).then_inc(signal.sem, 1)
            after(act, signal, t, signal.per - 1)
            s.activation(r, ln, ACT.Exp, scale=-0.5).then_inc(signal.sem, 1)

        def bounds(n):
            unread = splits[n].slots[:, 0, 0:splits[n].n].bitcast(BF16)
            for k in range(KD):
                act.wait_ge(w_chunk[n][k], 16)
                if k:
                    act.wait_ge(l1_done[n], k)
                s.activation(unread, splits[n].raw(k), ACT.Abs,
                             accum_out=l1[:, which_of[n], k:k + 1]).then_inc(l1_done[n], 1)

        def split_hi(n, chunks):
            w = splits[n]
            act.wait_ge(scaled[n], 1)
            for k in chunks:
                for part in range(2):
                    lo, hi = w.cols(part)
                    if k:
                        act.wait_ge(lo_done[n], 2 * (k - 1) + part + 1)
                    s.activation(w.half(0, k, lo, hi - lo), w.raw(k, lo, hi), ACT.Copy,
                                 scale=g_of[n][:, k:k + 1]).then_inc(hi_done[n], 1)
                if n == "in":
                    if k == 0:
                        act.wait_ge(band_ps, HEADS)
                    act.wait_ge(hi_done[n], 2 * k + 1)
                    s.activation(w_sq[:, k, :], w.half(0, k, O_V, KV * HD), ACT.Square, scale=2.0 ** -15).then_inc(v_sq, 1)

        s.preload_act_table_set("natural_log_exp_and_others")
        act.wait_ge(cst_in, 16)

        def body(t):
            proj, attn, route = live(t + 1, 0), live(t, 1), live(t - 1, 1)
            full = proj and live(t + 1, 1)
            if proj:
                after(act, pb, t)
                after(act, ph, t)
                for b, ps in enumerate((psE, psF)):
                    after(act, xT_ps, t + 1, b + 1)
                    s.activation(xT_hi[:, 4 * b:4 * b + 4, :].rearrange("p k c -> p (k c)"), ps[:, :], ACT.Copy,
                                 scale=XS).then_inc(xTh.sem, 1)
            if isinstance(t, int) and t == -1:
                split_hi("in", range(KD))
            if isinstance(t, int) and t == 0:
                bounds("out")
            if attn:
                for hd in range(HEADS):
                    if hd % 2 == 0:
                        after(act, n_top, t, hd // 2 + 1)
                    s.activation(prob[:, hd, :], prob[:, hd, :], ACT.Exp, bias=ntop[:, hd:hd + 1],
                                 accum_out=psum_[:, hd:hd + 1]).then_inc(p_sb.sem, 1)
                after(act, sink_ds, t)
                s.activation(sink_e, sink_d, ACT.Exp).then_inc(sink_es.sem, 1)
            if isinstance(t, int) and t == 1:
                split_hi("out", LAST_CHUNKS)
            if full:
                after(act, pq, t + 1)
                after(act, q_lo, t)
                s.activation(qsq[:], psG[:, :], ACT.Square, scale=inv_in).then_inc(q_sq.sem, 1)
            if attn:
                for b, ps in enumerate((psA, psB, psC, psD)):
                    after(act, pT_ps, t, b + 1)
                    after(act, o_ps, t - 1)
                    s.activation(probT_hi[:, 2 * b:2 * b + 2].rearrange("p a c q -> p (a c q)"), ps[:, :],
                                 ACT.Copy, scale=PS).then_inc(pT_act.sem, 1)
            if full:
                after(act, q_ss, t + 1)
                rstd(q_rs, t + 1, ss_q, ln_q, r_q, HD)
            if proj:
                after(act, pkv, t + 1)
                after(act, k_ss, t)
                s.activation(ksq[:], psH[:, 0:P], ACT.Square, scale=inv_in).then_inc(k_sq.sem, 1)
                if isinstance(t, int) and t == -1:
                    act.wait_ge(v_bound, 2)
                    s.activation(v_root, v_max, ACT.Ln).then_inc(v_rooted, 1)
                    act.wait_ge(v_rooted, 1)
                    s.activation(v_root, v_root, ACT.Exp, scale=0.5).then_inc(v_rooted, 1)
                    act.wait_ge(v_scaled, 5)
                after(act, v_cur, t)
                s.activation(vst[:, :, 0, :], psH[:, P:2 * P].rearrange("p (h d) -> p h d", h=KV), ACT.Copy,
                             scale=v_scale).then_inc(v_hi.sem, 1)
                after(act, k_ss, t + 1)
                after(act, k_n, t)
                rstd(k_rs, t + 1, ss_k, ln_k, r_k, HD)
            if attn:
                after(act, cv, t)
                s.activation(dump[:, 0:CC], yc[:], ACT.Square, accum_out=ss_c).then_inc(c_rs.sem, 1)
                after(act, c_rs, t, 1)
                after(act, c_n, t - 1)
                rstd(c_rs, t, ss_c, ln1[2], r_c, CC)
                after(act, c_rs, t)
                s.activation(yc[:], yc[:], ACT.Copy, scale=r_c).then_inc(c_n.sem, 1)
                after(act, a_s, t)
                s.activation(dump[:, 0:AD], a[:], ACT.Square, accum_out=ss_a).then_inc(a_rs.sem, 1)
                after(act, a_rs, t, 1)
                after(act, a_n, t - 1)
                rstd(a_rs, t, ss_a, ln1[1], r_a, AD)
                after(act, a_rs, t)
                s.activation(a[:], a[:], ACT.Copy, scale=r_a).then_inc(a_n.sem, 1)
            if full:
                after(act, q_n, t + 1)
                after(act, qT_ps, t)
                s.activation(q2[:, :, 0, :], qn[:].rearrange("p (h d) -> p h d", h=HEADS), ACT.Copy).then_inc(q_hi.sem, 1)
            if proj:
                after(act, pc, t + 1)
                after(act, u_s, t)
                s.activation(Cs[:], psF[:, :], ACT.Copy, scale=inv_in).then_inc(c_sb.sem, 1)
            if isinstance(t, int) and t == 0:
                split_hi("out", FIRST_CHUNKS)
            if attn:
                after(act, h_ps, t - 1)
                for i, ps in enumerate((psA, psB)):
                    after(act, mT_ps, t, i + 1)
                    s.activation(mT_hi[:, 4 * i:4 * i + 4, :].rearrange("p k c -> p (k c)"), ps[:, :], ACT.Copy,
                                 scale=XS).then_inc(mTh.sem, 1)
            if live(t + 2, 0):
                after(act, x_in, t + 2)
                after(act, x_rs, t + 1)
                s.activation(dump[:], xt[:], ACT.Square, accum_out=ss_x).then_inc(x_rs.sem, 1)
                after(act, x_rs, t + 2, 1)
                rstd(x_rs, t + 2, ss_x, ln1[0], r_x, D)
                after(act, x_rs, t + 2)
                s.activation(xt[:], xt[:], ACT.Copy, scale=r_x).then_inc(xn_s.sem, 1)
            if route:
                after(act, rt1, t - 1, 4)
                s.activation(rs[:, 20:24], lgb[:, 0:GROUPS], ACT.Exp, bias=rs[:, 1:2],
                             accum_out=rs[:, 2:3]).then_inc(rt_e.sem, 1)
            if route:
                after(act, rt1, t - 1, 18)
                s.activation(rs[:, 12:13], rs[:, 11:12], ACT.Exp).then_inc(rt_e.sem, 1)
            if attn:
                after(act, h_s, t)
                s.activation(dump[:], h[:], ACT.Square, accum_out=ss_h).then_inc(h_rs.sem, 1)
                after(act, h_rs, t, 1)
                after(act, hn_s, t - 1)
                rstd(h_rs, t, ss_h, ln1[3], r_h, D)
            if full:
                after(act, pb, t + 1)
                after(act, cv, t)
                if isinstance(t, int) and t == 0:
                    act.wait_ge(band_out, 16 * len(band_places))
                s.activation(Bs[:], psG[:, :], ACT.Copy, scale=inv_in).then_inc(b_sb.sem, 1)
                after(act, qT_ps, t + 1, 1)
                after(act, s_ps, t)
                s.activation(qT[:, 0:4 * P], psF[:, :], ACT.Copy).then_inc(qT_act.sem, 1)
            if attn:
                after(act, lg_ps, t - 1)
                for b, ps in enumerate((psC, psD)):
                    after(act, hT_ps, t, b + 1)
                    s.activation(hnT_hi[:, 4 * b:4 * b + 4, :].rearrange("p k c -> p (k c)"), ps[:, :], ACT.Copy,
                                 scale=hn_scale).then_inc(hT_act.sem, 1)
            if isinstance(t, int) and t == -2:
                bounds("in")
        schedule(act, body)

    @block.gpsimd
    def _(pool):
        g = nc.gpsimd
        g.memset(xt[:], 0.0).then_inc(blank.sem, 1)
        g.memset(xres[:], 0.0).then_inc(pool_step, 1)
        g.memset(yc[:], 0.0).then_inc(pool_step, 1)
        pool.wait_ge(pool_step, 2)
        fill = xres[:].bitcast(I32).rearrange("p (r j w) -> p r j w", r=4, w=2)
        pool.iota(fill[:, :, :, 0], pattern=[[0, 4], [1, P]], base=SEQ, channel_multiplier=0).then_inc(pool_step, 1)
        pool.wait_ge(pool_step, 3)
        def all_partitions(n):
            pool.wait_ge(bound[n], 2 if n == "out" else 1)
            w = which_of[n]
            pool.partition_all_reduce(scale_w[:, 2 + w:3 + w], scale_w[:, w:w + 1], P, RMAX).then_inc(all_bound[n], 1)

        all_partitions("in")
        for part in range(2):
            pool.dma_start(table[part * E * CAP // 2:(part + 1) * E * CAP // 2].rearrange("(p r) w -> p (r w)", p=P),
                           fill.rearrange("p r j w -> p (r j w)")).then_inc(filled, 16)
        for c in range(2):
            pool.dma_start(hn_dram[SEQ:SEQ + P, c * CC:(c + 1) * CC], yc[:]).then_inc(zeroed, 16)
            pool.dma_start(out[SEQ:SEQ + P, c * CC:(c + 1) * CC], yc[:]).then_inc(zeroed, 16)
        pool.wait_ge(band_sb, HEADS)
        for place, head, n in band_places:
            pool.dma_start(band_dram[:, head * BW:(head + n) * BW], place[:, 0:n * BW]).then_inc(band_out, 16)

        pool.wait_ge(band_out, 16 * len(band_places))
        pool.dma_start(bias[:], bass.AP(band_dram.tensor, band_dram.offset + P - 1,
                                        [[HEADS * BW - 1, P], [BW, HEADS], [1, 2 * P]])).then_inc(band_in, 16)
        pool.wait_ge(bound["out"], 1)
        pool.partition_all_reduce(rt_stat[:, 2:3], rt_stat[:, 0:1], P, RMAX).then_inc(all_bound["out"], 1)
        pool.wait_ge(zeroed, 64)
        pool.wait_ge(band_in, 16)

        def body(t):
            proj, attn, route = live(t + 1, 0), live(t, 1), live(t - 1, 1)
            if isinstance(t, int) and t == 1:
                pool.wait_ge(small_in, 16 * 21)
            if attn:
                after(pool, um_in, t)
                after(pool, u_s, t)
                after(pool, mT_ps, t - 1)
                g.tensor_tensor(yc[:], u[:], w_cv[:, 2, :], ALU.mult).then_inc(cv.sem, 1)
                g.tensor_tensor(um[:, 0, :], um[:, 0, :], w_cv[:, 1, :], ALU.mult).then_inc(cv.sem, 1)
                g.tensor_tensor(um[:, 1, :], um[:, 1, :], w_cv[:, 0, :], ALU.mult).then_inc(cv.sem, 1)
                after(pool, cv, t, 3)
                g.tensor_tensor(yc[:], yc[:], um[:, 0, :], ALU.add).then_inc(cv.sem, 1)
                after(pool, cv, t, 4)
                g.tensor_tensor(yc[:], yc[:], um[:, 1, :], ALU.add).then_inc(cv.sem, 1)
                after(pool, cv, t, 5)
                after(pool, b_sb, t)
                g.tensor_tensor(yc[:], yc[:], Bs[:], ALU.mult).then_inc(cv.sem, 1)
            if proj:
                if live(t + 1, 1):
                    after(pool, o_ps, t)
                    after(pool, v_cur, t)
                    hold(pool, pool_held)
                    g.tensor_copy(V[:, 0, :], V[:, 1, :]).then_inc(v_prev.sem, 1)
                    after(pool, v_prev, t + 1)
                after(pool, v_st, t + 1)
                hold(pool, pool_held)
                g.tensor_copy(V[:, 1, :], vst[:]).then_inc(v_cur.sem, 1)
            if isinstance(t, int) and t == 0:
                all_partitions("out")
            if route:
                after(pool, rt2, t - 1)
                hold(pool, pool_held)
                for n in range(2):
                    g.indirect_dma_start(table, bass.IndirectOffsetOnAxis(ap=slot[:, n:n + 1], axis=0),
                                         entry[:, n, :], None, bounds_check=E * CAP - 1).then_inc(listed.sem, 16)
        schedule(pool, body)
        after(pool, listed, TILES)

    @block.vector
    def _(dve):
        v = nc.vector
        steps = [0]

        def set_up(ins):
            steps[0] += 1
            ins.then_inc(dve_step, 1)
            dve.wait_ge(dve_step, steps[0])

        dve.wait_ge(cst_in, 16)
        set_up(v.tensor_copy(tri16[:], cst[:, C_TRI:C_TRI + P]))
        set_up(v.tensor_copy(one16[:], cst[:, C_ONE:C_ONE + P]))
        set_up(v.tensor_copy(running[:], cst[:, C_SLOT:C_SLOT + E]))
        set_up(v.tensor_copy(tok[:], cst[:, C_TOK:C_TOK + 1]))
        set_up(v.memset(pad_mask, 0.0))
        set_up(v.memset(pad_mask[:, 0:P - N_META], NEG))
        dve.wait_ge(hot_in, 32)
        v.memset(rb[BUCKETS:BUCKETS + 1, :], 1.0).then_inc(spread, 1)
        dve.wait_ge(spread, 1)
        for n in range(2):
            v.tensor_copy(rbx[n][0:BUCKETS + 1, :].rearrange("p (j c) -> p j c", j=4),
                          rb[:, 4 * n:4 * n + 4].unsqueeze(2).to_broadcast([BUCKETS + 1, 4, P])).then_inc(spread, 1)
        for place, head, n in band_places:
            for j in range(n):
                dve.wait_ge(band_ps, head + j + 1)
                v.tensor_copy(place[:, j * BW:(j + 1) * BW], banks[head + j][:, 0:BW]).then_inc(band_sb, 1)

        def scale_of_values():
            dve.wait_ge(v_cols, 1)
            v.tensor_reduce(v_max, psG[:, 0:P], AX, ALU.max).then_inc(v_bound, 1)
            dve.wait_ge(v_bound, 1)
            v.tensor_scalar(v_max, v_max, 1e-35, None, ALU.max).then_inc(v_bound, 1)
            dve.wait_ge(v_rooted, 2)
            v.tensor_scalar(sI[:, 4:5], v_root.bitcast(I32), 0x7F800000, None, ALU.bitwise_and).then_inc(v_scaled, 1)
            dve.wait_ge(v_scaled, 1)
            v.tensor_scalar(sI[:, 5:6], sI[:, 4:5], float(30 << 23), None, ALU.max).then_inc(v_scaled, 1)
            dve.wait_ge(v_scaled, 2)
            v.tensor_scalar(v_scale.bitcast(I32), sI[:, 5:6], -1.0, float(239 << 23), ALU.mult, ALU.add).then_inc(v_scaled, 1)
            v.tensor_scalar(inv_v.bitcast(I32), sI[:, 5:6], float(1 << 23), None, ALU.add).then_inc(v_scaled, 1)
            dve.wait_ge(v_scaled, 4)
            v.tensor_scalar(inv_v, inv_v, inv_in, None, ALU.mult).then_inc(v_scaled, 1)
            dve.wait_ge(v_scaled, 5)

        def scales_of_router():
            dve.wait_ge(small_in, 16 * 21)
            flat = w_rt[:].rearrange("p k n -> p (k n)")
            for n, (values, width) in enumerate(((flat, KD * RT), (g_ffn[:], D))):
                negative = h[:, 0:width]
                set_up(v.tensor_scalar(negative, values, -1.0, None, ALU.mult))
                set_up(v.tensor_reduce(rt_stat[:, 4 + n:5 + n], values, AX, ALU.max))
                set_up(v.tensor_reduce(rt_stat[:, 6 + n:7 + n], negative, AX, ALU.max))
            set_up(v.tensor_tensor(rt_stat[:, 0:2], rt_stat[:, 4:6], rt_stat[:, 6:8], ALU.max))
            v.tensor_copy(rt_stat[:, 3:4], rt_stat[:, 1:2]).then_inc(bound["out"], 1)
            dve.wait_ge(bound["out"], 1)
            dve.wait_ge(all_bound["out"], 1)
            set_up(v.tensor_scalar(sI[:, 0:2], rt_stat[:, 2:4].bitcast(I32), 0x7F800000, None, ALU.bitwise_and))
            set_up(v.tensor_scalar(sI[:, 2:4], sI[:, 0:2], float(30 << 23), None, ALU.max))
            w_scale = rt_stat[:, 5:6]
            set_up(v.tensor_scalar(w_scale.bitcast(I32), sI[:, 2:3], -1.0, float(268 << 23), ALU.mult, ALU.add))
            set_up(v.tensor_scalar(hn_scale.bitcast(I32), sI[:, 3:4], -1.0, float(263 << 23), ALU.mult, ALU.add))
            set_up(v.tensor_scalar(rt_stat[:, 6:7].bitcast(I32), sI[:, 2:3], float(-(14 << 23)), None, ALU.add))
            set_up(v.tensor_scalar(inv_rt.bitcast(I32), sI[:, 3:4], float(-(9 << 23)), None, ALU.add))
            set_up(v.tensor_scalar(inv_rt, inv_rt, rt_stat[:, 6:7], None, ALU.mult))
            set_up(v.tensor_scalar(w_rt16[:, :, 0, :], w_rt[:], w_scale, None, ALU.mult))
            set_up(v.scalar_tensor_tensor(w_rt16[:, :, 1, :], w_rt[:], w_scale, w_rt16[:, :, 0, :], ALU.mult, ALU.subtract))

        def scale_of(n):
            c = which_of[n]
            mine, inverse, power = (scale_w[:, q + c:q + c + 1] for q in (0, 4, 6))
            dve.wait_ge(l1_done[n], KD)
            set_up(v.tensor_tensor(l1[:, c, 0:KD], l1[:, c, 0:KD], g_of[n][:], ALU.mult))
            set_up(v.tensor_scalar(l1[:, c, KD:], l1[:, c, 0:KD], -1.0, None, ALU.mult))
            v.tensor_reduce(mine, l1[:, c, :], AX, ALU.max).then_inc(bound[n], 1)
            dve.wait_ge(all_bound[n], 2 if n == "out" else 1)
            set_up(v.tensor_scalar(sI[:, c:c + 1], scale_w[:, 2 + c:3 + c].bitcast(I32), 0x7F800000, None, ALU.bitwise_and))
            set_up(v.tensor_scalar(sI[:, 2 + c:3 + c], sI[:, c:c + 1], float(30 << 23), None, ALU.max))
            set_up(v.tensor_scalar(power.bitcast(I32), sI[:, 2 + c:3 + c], -1.0, float(268 << 23), ALU.mult, ALU.add))
            set_up(v.tensor_scalar(inverse.bitcast(I32), sI[:, 2 + c:3 + c], float(-(22 << 23)), None, ALU.add))
            v.tensor_scalar(g_of[n][:], g_of[n][:], power, None, ALU.mult).then_inc(scaled[n], 1)
            dve.wait_ge(scaled[n], 1)

        def split_lo(n, chunks):
            w = splits[n]
            for k in chunks:
                for part in range(2):
                    lo, hi = w.cols(part)
                    dve.wait_ge(hi_done[n], 2 * k + part + 1)
                    v.scalar_tensor_tensor(w.half(1, k, lo, hi - lo), w.raw(k, lo, hi), g_of[n][:, k:k + 1],
                                           w.half(0, k, lo, hi - lo), ALU.mult, ALU.subtract).then_inc(lo_done[n], 1)

        def body(t):
            proj, attn, route = live(t + 1, 0), live(t, 1), live(t - 1, 1)
            full = proj and live(t + 1, 1)

            def lo_half(out, ps, hi, signal):
                v.scalar_tensor_tensor(out.rearrange("p k c -> p (k c)"), ps[:, :], XS,
                                       hi.rearrange("p k c -> p (k c)"), ALU.mult, ALU.subtract).then_inc(signal.sem, 1)

            if proj:
                after(dve, pb, t)
                after(dve, ph, t)
                for b, ps in enumerate((psE, psF)):
                    after(dve, xTh, t + 1, b + 1)
                    lo_half(xT_lo[:, 4 * b:4 * b + 4, :], ps, xT_hi[:, 4 * b:4 * b + 4, :], xTl)
            if isinstance(t, int) and t == -1:
                dve.wait_ge(g_in, 16 * 7)
                set_up(v.scalar_tensor_tensor(g_qk[:, 0:1], gk[:, 0:1], HD ** -0.5, gk[:, 1:2], ALU.mult, ALU.mult))
                scale_of("in")
                split_lo("in", range(KD))
            if isinstance(t, int) and t == 0:
                scales_of_router()
            if isinstance(t, int) and t == 1:
                dve.wait_ge(band_in, 16)
            if attn:
                after(dve, pT_ps, t - 1)
                after(dve, sink_es, t - 1)
                after(dve, den_s, t - 1)
                for j, ps in enumerate((psA, psB, psC, psD)):
                    after(dve, s_ps, t, j + 1)
                    hold(dve, dve_held)
                    for i in range(2):
                        hd = 2 * j + i
                        v.tensor_tensor_reduce(prob[:, hd, :], ps[:, i * 256:(i + 1) * 256], bias[:, hd, :], 1.0,
                                               sinks[:, hd:hd + 1], ALU.add, ALU.max,
                                               top[:, hd:hd + 1]).then_inc(s_sb.sem, 1)
                    after(dve, s_sb, t, 2 * j + 2)
                    v.tensor_scalar(ntop[:, 2 * j:2 * j + 2], top[:, 2 * j:2 * j + 2], -1.0, None,
                                    ALU.mult).then_inc(n_top.sem, 1)
                after(dve, n_top, t)
                v.tensor_tensor(sink_d, sinks[:], ntop, ALU.add).then_inc(sink_ds.sem, 1)
            if isinstance(t, int) and t == 1:
                split_lo("out", LAST_CHUNKS)
            if route:
                n1 = [0]

                def step(ins):
                    n1[0] += 1
                    ins.then_inc(rt1.sem, 1)
                    after(dve, rt1, t - 1, n1[0])

                w4, w32 = cst[:, C_W4:C_W4 + GROUPS], cst[:, C_W32:C_W32 + E]
                gm, ngm, m4, v1, m1, v2, m2 = (rs[:, c:c + 1] for c in (0, 1, 3, 4, 5, 6, 7))
                after(dve, lg_ps, t - 1)
                step(v.scalar_tensor_tensor(lgb[:], psH[:, 256 + RT:256 + 2 * RT], inv_rt, b_rt[:], ALU.mult, ALU.add))
                step(v.scalar_tensor_tensor(lgb[:], psH[:, 256:256 + RT], inv_rt, lgb[:], ALU.mult, ALU.add))
            if attn:
                for b, ps in enumerate((psA, psB, psC, psD)):
                    after(dve, pT_act, t, b + 1)
                    v.scalar_tensor_tensor(probT_lo[:, 2 * b:2 * b + 2].rearrange("p a c q -> p (a c q)"), ps[:, :], PS,
                                           probT_hi[:, 2 * b:2 * b + 2].rearrange("p a c q -> p (a c q)"),
                                           ALU.mult, ALU.subtract).then_inc(pT_dve.sem, 1)
                after(dve, sink_es, t)
                after(dve, p_sb, t)
                v.tensor_tensor(den, psum_, sink_e, ALU.add).then_inc(den_s.sem, 1)
                after(dve, den_s, t, 1)
                v.reciprocal(den, den).then_inc(den_s.sem, 1)
                after(dve, den_s, t, 2)
                v.tensor_scalar(den, den, inv_v, None, ALU.mult).then_inc(den_s.sem, 1)
            if full:
                after(dve, kT_s, t)
                after(dve, s_ps, t)
                v.tensor_copy(kT[:, :, :, 0:P], kT[:, :, :, P:]).then_inc(k_prev.sem, 1)
                after(dve, q_sq, t + 1)
                after(dve, q_rs, t)
                v.tensor_reduce(ss_q, qsq[:].rearrange("p (h d) -> p h d", h=HEADS), AX, ALU.add).then_inc(q_ss.sem, 1)
            if proj:
                after(dve, k_sq, t + 1)
                after(dve, k_rs, t)
                v.tensor_reduce(ss_k, ksq[:].rearrange("p (h d) -> p h d", h=KV), AX, ALU.add).then_inc(k_ss.sem, 1)
                if isinstance(t, int) and t == -1:
                    scale_of_values()
                after(dve, v_hi, t + 1)
                v.scalar_tensor_tensor(vst[:, :, 1, :], psH[:, P:2 * P].rearrange("p (h d) -> p h d", h=KV), v_scale,
                                       vst[:, :, 0, :], ALU.mult, ALU.subtract).then_inc(v_st.sem, 1)
            if attn:
                after(dve, o_ps, t)
                after(dve, den_s, t)
                after(dve, mT_ps, t - 1)
                a_heads = a[:].rearrange("p (h d) -> p h d", h=HEADS)
                for kv, ps in enumerate((psE, psA)):
                    o = ps[:, :].rearrange("p (h a d) -> p h a d", h=4, a=2)
                    v.tensor_copy(a_heads[:, 4 * kv:4 * kv + 4, :], o[:, :, 1, :]).then_inc(o_lo.sem, 1)
                    after(dve, o_lo, t, kv + 1)
                    v.tensor_tensor(a_heads[:, 4 * kv:4 * kv + 4, :], o[:, :, 0, :], a_heads[:, 4 * kv:4 * kv + 4, :],
                                    ALU.add).then_inc(a_s.sem, 1)
                after(dve, a_s, t, 2)
                v.tensor_tensor(a_heads, a_heads, den.unsqueeze(2).to_broadcast([P, HEADS, HD]), ALU.mult).then_inc(a_s.sem, 1)
            if full:
                after(dve, q_rs, t + 1)
                v.scalar_tensor_tensor(qn[:].rearrange("p (h d) -> p h d", h=HEADS),
                                       psG[:, :].rearrange("p (h d) -> p h d", h=HEADS), inv_in,
                                       r_q.unsqueeze(2).to_broadcast([P, HEADS, HD]),
                                       ALU.mult, ALU.mult).then_inc(q_n.sem, 1)
            if proj:
                after(dve, k_rs, t + 1)
                after(dve, kT_ps, t)
                for copy in range(2):
                    v.scalar_tensor_tensor(kn[:, :, copy, :],
                                           psH[:, 0:P].rearrange("p (h d) -> p h d", h=KV), inv_in,
                                           r_k.unsqueeze(2).to_broadcast([P, KV, HD]),
                                           ALU.mult, ALU.mult).then_inc(k_n.sem, 1)
            if full:
                after(dve, q_hi, t + 1)
                after(dve, qT_ps, t)
                v.tensor_tensor(q2[:, :, 1, :], qn[:].rearrange("p (h d) -> p h d", h=HEADS),
                                q2[:, :, 0, :].bitcast(F32), ALU.subtract).then_inc(q_lo.sem, 1)
            if route:
                step(v.tensor_reduce(gm, lgb[:, 0:GROUPS], AX, ALU.max))
                step(v.tensor_scalar(ngm, gm, -1.0, None, ALU.mult))
                step(v.scalar_tensor_tensor(cand[:, 0:GROUPS], lgb[:, 0:GROUPS], gm, w4, ALU.is_equal, ALU.mult))
                step(v.tensor_reduce(m4, cand[:, 0:GROUPS], AX, ALU.max))
                step(v.tensor_scalar(oh4[:], w4, m4, None, ALU.is_equal))
                step(v.tensor_scalar(pen4[:], oh4[:], -NEG, NEG, ALU.mult, ALU.add))
                step(v.tensor_tensor(lm[:].rearrange("p (g e) -> p g e", g=GROUPS),
                                     lgb[:, GROUPS:].rearrange("p (g e) -> p g e", g=GROUPS),
                                     pen4[:].unsqueeze(2).to_broadcast([P, GROUPS, PER_GROUP]), ALU.add))
            if attn:
                after(dve, h_ps, t - 1)
                for i, ps in enumerate((psA, psB)):
                    after(dve, mTh, t, i + 1)
                    lo_half(mT_lo[:, 4 * i:4 * i + 4, :], ps, mT_hi[:, 4 * i:4 * i + 4, :], mTl)
            if route:
                step(v.tensor_reduce(v1, lm[:], AX, ALU.max))
                step(v.scalar_tensor_tensor(cand[:], lm[:], v1, w32, ALU.is_equal, ALU.mult))
                step(v.tensor_reduce(m1, cand[:], AX, ALU.max))
                step(v.tensor_scalar(hot1[:], w32, m1, None, ALU.is_equal))
                step(v.scalar_tensor_tensor(lm[:], hot1[:], -3e38, lm[:], ALU.mult, ALU.add))
                step(v.tensor_reduce(v2, lm[:], AX, ALU.max))
                step(v.scalar_tensor_tensor(cand[:], lm[:], v2, w32, ALU.is_equal, ALU.mult))
                step(v.tensor_reduce(m2, cand[:], AX, ALU.max))
                step(v.tensor_tensor(rs[:, 11:12], v2, v1, ALU.subtract))
                v.tensor_scalar(hot2[:], w32, m2, None, ALU.is_equal).then_inc(hot2_s.sem, 1)
                after(dve, hot2_s, t - 1)
                after(dve, cnt_ps, t - 2)
                step(v.tensor_tensor(both16[:], hot1[:], hot2[:], ALU.add))
            if isinstance(t, int) and t == 0:
                scale_of("out")
                split_lo("out", FIRST_CHUNKS)
            if proj:
                after(dve, ph, t + 1)
                after(dve, c_sb, t + 1)
                after(dve, u_out, t)
                after(dve, cv, t, 1)
                v.scalar_tensor_tensor(u[:], psC[:, :], inv_in, Cs[:], ALU.mult, ALU.mult).then_inc(u_s.sem, 1)
            if route:
                n2 = [0]

                def step2(ins):
                    n2[0] += 1
                    ins.then_inc(rt2.sem, 1)
                    after(dve, rt2, t - 1, n2[0])

                gp, ed, one_ed = rs[:, 13:14], rs[:, 12:13], rs[:, 14:15]
                gates = entry[:].bitcast(F32)
                after(dve, listed, t - 2)
                after(dve, rt_e, t - 1)
                step2(v.reciprocal(gp, rs[:, 2:3]))
                step2(v.tensor_scalar(one_ed, ed, 1.0, None, ALU.add))
                step2(v.reciprocal(one_ed, one_ed))
                step2(v.tensor_tensor(gates[:, 0, 1:2], gp, one_ed, ALU.mult))
                step2(v.tensor_tensor(gates[:, 1, 1:2], gates[:, 0, 1:2], ed, ALU.mult))
                after(dve, cnt_ps, t - 1)
                step2(v.tensor_tensor(rank[:], psH[:, 384:416], running[:], ALU.add))
                v.tensor_tensor_reduce(cand[:], hot1[:], rank[:], 1.0, 0.0, ALU.mult, ALU.add, rs[:, 16:17]).then_inc(rt2.sem, 1)
                v.tensor_tensor_reduce(lm[:], hot2[:], rank[:], 1.0, 0.0, ALU.mult, ALU.add, rs[:, 17:18]).then_inc(rt2.sem, 1)
                n2[0] += 2
                after(dve, rt2, t - 1, n2[0])
                v.tensor_tensor(running[:], running[:], psH[:, 416:448], ALU.add).then_inc(counted.sem, 1)
                v.tensor_copy(entry[:, :, 0], tok[:].to_broadcast([P, 2])).then_inc(counted.sem, 1)
                after(dve, counted, t - 1)
                step2(v.tensor_copy(slot[:], rs[:, 16:18]))
                step2(v.tensor_scalar(tok[:], tok[:], float(P), None, ALU.add))
                assert n2[0] == R2
            if attn:
                after(dve, xres_in, t)
                after(dve, rows_out, t - 1)
                for n, ps in enumerate((psD, psE)):
                    after(dve, h_ps, t, n + 1)
                    c = slice(n * 512, (n + 1) * 512)
                    v.scalar_tensor_tensor(h[:, c], ps[:, :], inv_out, xres[:, c], ALU.mult, ALU.add).then_inc(h_s.sem, 1)
                after(dve, h_s, t)
                after(dve, h_rs, t)
                after(dve, hT_ps, t - 1)
                v.scalar_tensor_tensor(hn[:], h[:], r_h, g_ffn[:], ALU.mult, ALU.mult).then_inc(hn_s.sem, 1)
            if full:
                after(dve, k_prev, t + 1)
            if proj:
                after(dve, kT_ps, t + 1)
                keys, (k_hi, k_lo) = psH[:, 0:2 * P].rearrange("p (h k) -> p h k", h=KV), (kT[:, n, :, P:] for n in range(2))
                v.tensor_scalar(k_hi, keys, g_qk[:, 0:1], None, ALU.mult).then_inc(kT_hi.sem, 1)
                after(dve, kT_hi, t + 1)
                v.scalar_tensor_tensor(k_lo, keys, g_qk[:, 0:1], k_hi.bitcast(F32), ALU.mult, ALU.subtract
                                       ).then_inc(kT_s.sem, 1)
            if full:
                after(dve, qT_ps, t + 1)
                v.tensor_copy(qT[:, 4 * P:], psB[:, :]).then_inc(qT_dve.sem, 1)
            if attn:
                for b, ps in enumerate((psC, psD)):
                    after(dve, hT_act, t, b + 1)
                    v.scalar_tensor_tensor(hnT_lo[:, 4 * b:4 * b + 4, :].rearrange("p k c -> p (k c)"), ps[:, :], hn_scale,
                                           hnT_hi[:, 4 * b:4 * b + 4, :].rearrange("p k c -> p (k c)"),
                                           ALU.mult, ALU.subtract).then_inc(hT_dve.sem, 1)

        schedule(dve, body)
        steps = [0]
        last = sig("last").sem

        def step(ins):
            steps[0] += 1
            ins.then_inc(last, 1)
            dve.wait_ge(last, steps[0])

        nb, ping, pong = hot1, hot2, rank
        counts = slice(0, E)
        step(v.tensor_tensor(nb[:], running[:], cst[:, C_SLOT:C_SLOT + E], ALU.subtract))
        step(v.tensor_scalar(blocks_of[:, counts], nb[:], float(P - 1), None, ALU.add))
        step(v.tensor_scalar(blocks_of[:, E:], blocks_of[:, counts], 7, None, ALU.arith_shift_right))
        step(v.tensor_scalar(blocks_of[:, counts], blocks_of[:, E:], 1, None, ALU.max))
        step(v.tensor_scalar(blocks_of[:, 0:1], blocks_of[:, 0:1], 2, None, ALU.max))
        step(v.tensor_copy(nb[:], blocks_of[:, counts]))
        step(v.tensor_copy(ping[:], nb[:]))
        shift = 1
        while shift < E:
            step(v.tensor_copy(pong[:, 0:shift], ping[:, 0:shift]))
            step(v.tensor_tensor(pong[:, shift:], ping[:, shift:], ping[:, 0:E - shift], ALU.add))
            ping, pong = pong, ping
            shift *= 2
        step(v.tensor_tensor(blocks_of[:, E:], ping[:], nb[:], ALU.subtract))



def experts(nc, ctx, env):
    out, table, hn_dram, cst, ident, blocks_of, raw, raw_in, load_expert = (env[n] for n in (
        "out table hn_dram cst ident blocks_of raw raw_in load_expert").split())
    psA, psB, psC, psD, psE, psF, psG = (env[f"ps{c}"] for c in "ABCDEFG")

    def sb(name, shape, dt=F32):
        return ctx.enter_context(nc.sbuf_tensor(name, shape, dt))

    def sem(name):
        return ctx.enter_context(nc.semaphore(name))

    hi = {n: sb(f"{n}_hi", [P, 8, 512], F32R) for n in raw}
    lo = {n: sb(f"{n}_lo", [P, 8, 512], F32R) for n in raw}
    xg = sb("xg", [P, D])
    gT_hi, gT_lo = sb("gT_hi", [P, KD, P], F32R), sb("gT_lo", [P, KD, P], F32R)
    gated, act_rows = sb("gated", [P, DE]), sb("act_rows", [P, DE])
    aT_hi, aT_lo = sb("aT_hi", [P, KE, P], F32R), sb("aT_lo", [P, KE, P], F32R)
    y = sb("y", [P, D])
    slots, slots_old = sb("slots", [P, 4, 2], I32), sb("slots_old", [P, 3, 2], I32)

    hi_s = {n: sem(f"hi_s_{n}") for n in raw}
    lo_s = {n: sem(f"lo_s_{n}") for n in raw}
    slots_in, moved, shifted, rows_in = sem("slots_in"), sem("moved"), sem("shifted"), sem("rows_in")
    xgT_ps, xgT_hi, xgT_lo = sem("xgT_ps"), sem("xgT_hi"), sem("xgT_lo")
    gate_ps, up_ps, silu_s, act_s = sem("gate_ps"), sem("up_ps"), sem("silu_s"), sem("act_s")
    aT_ps, aT_hi_s, aT_lo_s, y_ps = sem("aT_ps"), sem("aT_hi_s"), sem("aT_lo_s"), sem("y_ps")
    y_act, y_dve, added, cleared = sem("y_act"), sem("y_dve"), sem("added"), sem("cleared")
    held = sem("held")

    def walk(eng, block, before=None):
        def loads(e):
            n = eng.value_load(blocks_of[0:1, bass.ds(e, 1)], min_val=1, max_val=TILES)
            base = eng.value_load(blocks_of[0:1, bass.ds(e + E, 1)], min_val=0, max_val=3 * TILES)
            return n, base

        n, _ = loads(0)
        block(0, 0, 0, True)
        block(0, 1, 1, False)
        with eng.If(n > 2):
            with eng.Fori(2, n) as i:
                block(0, i, i, False)
        with eng.Fori(1, E) as e:
            n, base = loads(e)
            block(e, 0, base, True)
            with eng.If(n > 1):
                with eng.Fori(1, n) as i:
                    block(e, i, base + i, False)
        n, base = loads(E - 1)
        return base + n

    block = ctx.enter_context(nc.Block())

    @block.sync
    def _(sp):
        with sp.Fori(1, E) as e:
            for n in raw:
                sp.wait_ge(hi_s[n], 8 * e)
                sp.wait_ge(lo_s[n], 8 * e)
                load_expert(sp, n, e)

    @block.gpsimd
    def _(pool):
        g = nc.gpsimd

        def gather():
            pool.indirect_dma_start(xg[:], None, hn_dram, bass.IndirectOffsetOnAxis(ap=slots[:, 0, 0:1], axis=0),
                                    bounds_check=SEQ + P - 1).then_inc(rows_in, 16)

        def scatter(b):
            pool.wait_ge(y_act, b + 1)
            pool.wait_ge(y_dve, b + 1)
            hold(pool, held)
            pool.indirect_dma_start(out, bass.IndirectOffsetOnAxis(ap=slots[:, 3, 0:1], axis=0), y[:], None,
                                    compute_op=ALU.add, bounds_check=SEQ + P - 1).then_inc(added, 16)
            pool.wait_ge(added, 16 * b + 16)
            hold(pool, held)

        def shift(b):
            g.tensor_copy(slots_old[:], slots[:, 0:3, :]).then_inc(moved, 1)
            pool.wait_ge(moved, b + 1)
            hold(pool, held)
            g.tensor_copy(slots[:, 1:4, :], slots_old[:]).then_inc(shifted, 1)
            pool.wait_ge(shifted, b + 1)
            hold(pool, held)

        def block_(e, i, b, first):
            known = isinstance(b, int)
            if known and b == 0:
                pool.sem_inc(moved, 1)
                pool.sem_inc(shifted, 1)
            else:
                shift(b)
            pool.dma_start(slots[:, 0, :], table[bass.ds(e * CAP + i * P, P), :]).then_inc(slots_in, 16)
            pool.wait_ge(slots_in, 16 * (b + 1))
            if not (isinstance(b, int) and b == 0):
                pool.wait_ge(xgT_ps, 2 * b)
                hold(pool, held)
            gather()
            if known:
                pool.wait_ge(cleared, 3)
                pool.dma_start(out[SEQ + b:SEQ + b + 1, 0:8], y[0:1, 0:8]).then_inc(added, 16)
            else:
                scatter(b)
            pool.wait_ge(rows_in, 16 * (b + 1))
            hold(pool, held)
            if known and b == 1:
                pool.wait_ge(added, 32)

        pool.wait_ge(cleared, 2)
        total = walk(pool, block_)
        shift(total)
        pool.wait_ge(xgT_ps, 2 * total)
        hold(pool, held)
        gather()
        scatter(total)
        pool.wait_ge(rows_in, 16 * (total + 1))
        hold(pool, held)
        shift(total + 1)
        scatter(total + 1)
        shift(total + 2)
        scatter(total + 2)

    @block.tensor
    def _(pe):
        def split_mm(ps, l_k, left, right, r_k, fresh, name=None, e=0):
            for n, k in enumerate(l_k):
                if fresh:
                    pe.wait_ge(hi_s[name], e * 8 + r_k[n] + 1)
                    pe.wait_ge(lo_s[name], e * 8 + r_k[n] + 1)
                for j, (l, r) in enumerate(((left[0], right[0]), (left[0], right[1]), (left[1], right[0]))):
                    m = nc.tensor.matmul(ps[:, :], l[:, k, :], r[:, r_k[n], :], start=(n == 0 and j == 0),
                                         stop=(n == len(l_k) - 1 and j == 2))
            return m

        def transpose_rows(b):
            pe.wait_ge(rows_in, 16 * (b + 1))
            for h, ps in enumerate((psC, psD)):
                for c in range(4):
                    m = nc.tensor.transpose(ps[:, c * P:(c + 1) * P], xg[:, (4 * h + c) * P:(4 * h + c + 1) * P], ident)
                m.then_inc(xgT_ps, 1)

        def turn_act(b):
            pe.wait_ge(act_s, b)
            for c in range(KE):
                m = nc.tensor.transpose(psE[:, c * P:(c + 1) * P], act_rows[:, c * P:(c + 1) * P], ident)
            m.then_inc(aT_ps, 1)

        def down(b):
            pe.wait_ge(aT_hi_s, b)
            pe.wait_ge(aT_lo_s, b)
            pe.wait_ge(y_act, b + 2)
            pe.wait_ge(y_dve, b + 2)
            for half, ps in enumerate((psF, psG)):
                split_mm(ps, range(KE), (aT_hi, aT_lo), (hi["down"], lo["down"]), [2 * k + half for k in range(KE)],
                         False).then_inc(y_ps, 1)

        def block_(e, i, b, first):
            static0 = isinstance(b, int) and b == 0
            pe.wait_ge(xgT_hi, 2 * (b + 1))
            pe.wait_ge(xgT_lo, 2 * (b + 1))
            if not static0:
                pe.wait_ge(silu_s, b)
            split_mm(psA, range(KD), (gT_hi, gT_lo), (hi["gate"], lo["gate"]), list(range(KD)), first, "gate", e
                     ).then_inc(gate_ps, 1)
            if not static0:
                turn_act(b)
            split_mm(psB, range(KD), (gT_hi, gT_lo), (hi["up"], lo["up"]), list(range(KD)), first, "up", e
                     ).then_inc(up_ps, 1)
            transpose_rows(b + 1)
            if not static0:
                loaded = 8 * e if first else 8 * (e + 1)
                pe.wait_ge(hi_s["down"], loaded)
                pe.wait_ge(lo_s["down"], loaded)
                down(b)

        pe.sem_inc(y_ps, 4)
        transpose_rows(0)
        total = walk(pe, block_)
        turn_act(total)
        pe.wait_ge(hi_s["down"], 8 * E)
        pe.wait_ge(lo_s["down"], 8 * E)
        down(total)

    def halves(eng, split, copy_y, act_stage, turn, turn_x):
        def block_(e, i, b, first):
            known = isinstance(b, int)
            if first and not (known and b == 0):
                eng.wait_ge(gate_ps, b)
                split("gate", e)
            if not (known and b < 2):
                copy_y(b)
            if first:
                if not (known and b == 0):
                    eng.wait_ge(up_ps, b)
                split("up", e)
            if not (known and b == 0):
                turn(b)
            act_stage(b)
            turn_x(b + 1)
            if first:
                if not (known and b == 0):
                    eng.wait_ge(y_ps, 2 * b + 4)
                split("down", e)
        split("gate", 0)
        turn_x(0)
        total = walk(eng, block_)
        copy_y(total)
        turn(total)
        copy_y(total + 1)

    gate_of = slots[:, 3, 1:2].bitcast(F32)

    @block.scalar
    def _(act):
        s = nc.scalar

        def split(n, e):
            act.wait_ge(raw_in[n], 16 * (e + 1))
            for k in range(8):
                s.activation(hi[n][:, k, :], raw[n][:, k, :], ACT.Copy).then_inc(hi_s[n], 1)

        def copy_y(b):
            act.wait_ge(y_ps, 2 * b + 1)
            act.wait_ge(shifted, b + 2)
            act.wait_ge(added, 16 * b + 16)
            s.activation(y[:, 0:512], psF[:, :], ACT.Copy, scale=gate_of).then_inc(y_act, 1)

        def silu(b):
            act.wait_ge(gate_ps, b + 1)
            if not (isinstance(b, int) and b == 0):
                act.wait_ge(act_s, b)
            s.activation(gated[:], psA[:, :], ACT.Silu).then_inc(silu_s, 1)

        def turn(b):
            act.wait_ge(aT_ps, b)
            act.wait_ge(y_ps, 2 * b + 2)
            s.activation(aT_hi[:].rearrange("p k c -> p (k c)"), psE[:, :], ACT.Copy).then_inc(aT_hi_s, 1)

        def turn_x(b):
            if not (isinstance(b, int) and b == 0):
                act.wait_ge(up_ps, b)
            for h, ps in enumerate((psC, psD)):
                act.wait_ge(xgT_ps, 2 * b + h + 1)
                s.activation(gT_hi[:, 4 * h:4 * h + 4, :].rearrange("p k c -> p (k c)"), ps[:, :],
                             ACT.Copy).then_inc(xgT_hi, 1)

        s.preload_act_table_set("silu_and_others")
        act.sem_inc(y_act, 3)
        halves(act, split, copy_y, silu, turn, turn_x)

    @block.vector
    def _(dve):
        v = nc.vector

        def split(n, e):
            dve.wait_ge(raw_in[n], 16 * (e + 1))
            for k in range(8):
                dve.wait_ge(hi_s[n], e * 8 + k + 1)
                v.tensor_tensor(lo[n][:, k, :], raw[n][:, k, :], hi[n][:, k, :].bitcast(F32),
                                ALU.subtract).then_inc(lo_s[n], 1)

        def copy_y(b):
            dve.wait_ge(y_ps, 2 * b + 2)
            dve.wait_ge(shifted, b + 2)
            dve.wait_ge(added, 16 * b + 16)
            v.tensor_scalar(y[:, 512:], psG[:, :], gate_of, None, ALU.mult).then_inc(y_dve, 1)

        def product(b):
            dve.wait_ge(up_ps, b + 1)
            dve.wait_ge(silu_s, b + 1)
            if not (isinstance(b, int) and b == 0):
                dve.wait_ge(aT_ps, b)
            v.tensor_tensor(act_rows[:], psB[:, :], gated[:], ALU.mult).then_inc(act_s, 1)

        def turn(b):
            dve.wait_ge(aT_hi_s, b)
            v.tensor_tensor(aT_lo[:].rearrange("p k c -> p (k c)"), psE[:, :],
                            aT_hi[:].rearrange("p k c -> p (k c)").bitcast(F32), ALU.subtract).then_inc(aT_lo_s, 1)

        def turn_x(b):
            for h, ps in enumerate((psC, psD)):
                dve.wait_ge(xgT_hi, 2 * b + h + 1)
                v.tensor_tensor(gT_lo[:, 4 * h:4 * h + 4, :].rearrange("p k c -> p (k c)"), ps[:, :],
                                gT_hi[:, 4 * h:4 * h + 4, :].rearrange("p k c -> p (k c)").bitcast(F32),
                                ALU.subtract).then_inc(xgT_lo, 1)

        v.memset(slots[:], 0).then_inc(cleared, 1)
        dve.wait_ge(cleared, 1)
        v.tensor_copy(slots[:, :, 0], cst[:, C_JUNK:C_JUNK + 1].to_broadcast([P, 4])).then_inc(cleared, 1)
        v.memset(y[:], 0.0).then_inc(cleared, 1)
        dve.sem_inc(y_dve, 3)
        halves(dve, split, copy_y, product, turn, turn_x)


_INS = ['x', 'meta_tokens', 'rel_bias', 'mix_norm_g', 'w_in', 'q_norm_g', 'k_norm_g', 'attn_sinks', 'conv_w',
        'attn_out_norm_g', 'conv_out_norm_g', 'w_out', 'ffn_norm_g', 'w_group_router', 'b_group_router',
        'w_expert_router', 'b_expert_router', 'w_gate', 'w_up', 'w_down']


def kernel(**inputs):
    import concourse.bacc as bacc
    from concourse.bass_utils import run_bass_kernel_spmd

    nc = bacc.Bacc("TRN2", target_bir_lowering=False, num_devices=1)
    arrays, args = {}, []
    for name, a in [(n, inputs[n]) for n in _INS] + list(zip(("consts", "onehot"), constants())):
        a = np.ascontiguousarray(a)
        arrays[f"in_{name}"] = a
        args.append(nc.dram_tensor(f"in_{name}", a.shape, mybir.dt.from_np(a.dtype), kind="ExternalInput").ap())
    out = nc.dram_tensor("out_rows", (SEQ + P, D), F32, kind="ExternalOutput").ap()
    build(nc, *args, out)
    r = run_bass_kernel_spmd(nc, [arrays], core_ids=[0])
    return r.results[0]["out_rows"][:SEQ].reshape(1, SEQ, D)
```
